# Optimizing a Trainium2 kernel written in Bass

```python
import jax, jax.numpy as jnp
from jax import lax
import numpy as np

D_MODEL = 1024
BATCH = 1
SEQ = 512
DEPTH = 2

D_MIX = D_MODEL
D_RNN = D_MIX // 2
RNN_HEADS = 8
RNN_BLOCK = D_RNN // RNN_HEADS
CONV_WIDTH = 4
CONV_PAD = (2, 1)
LRU_C = 8.0
GLA_HEADS = 4
GLA_DV_TOTAL = D_MIX - D_RNN
GLA_DK_TOTAL = GLA_DV_TOTAL // 2
GLA_DV = GLA_DV_TOTAL // GLA_HEADS
GLA_DK = GLA_DK_TOTAL // GLA_HEADS
GLA_RANK = 16
GLA_TAU = 16.0
GLA_CHUNK = 64
D_FF = ((8 * D_MODEL + 2) // 3 + 255) // 256 * 256
D_IN = 2 * D_RNN + 2 * GLA_DK_TOTAL + 2 * GLA_DV_TOTAL + 2 * GLA_RANK
RMS_EPS = 1e-6

kernel_name = 'hymba_rglru_gla_encoder'

def rms_norm(x, gain):
    xf = x.astype(jnp.float32)
    y = xf * lax.rsqrt(jnp.mean(xf * xf, axis=-1, keepdims=True) + RMS_EPS)
    return (y * gain.astype(jnp.float32)).astype(x.dtype)

def centred_depthwise_conv(x, w, b):
    y = lax.conv_general_dilated(
        x, w[:, None, :], window_strides=(1,), padding=[CONV_PAD],
        dimension_numbers=('NWC', 'WIO', 'NWC'), feature_group_count=x.shape[-1])
    return y + b

def linear_scan(a, u, reverse):
    def combine(c1, c2):
        a1, b1 = c1
        a2, b2 = c2
        return a1 * a2, a2 * b1 + b2
    _, h = lax.associative_scan(combine, (a, u), axis=1, reverse=reverse)
    return h

def rg_lru(x, w_a, b_a, w_x, b_x, lam, reverse):
    B, S, _ = x.shape
    xf = x.astype(jnp.float32)
    xh = xf.reshape(B, S, RNN_HEADS, RNN_BLOCK)
    r = jax.nn.sigmoid(jnp.einsum('bshi,hij->bshj', xh, w_a.astype(jnp.float32)).reshape(B, S, D_RNN) + b_a)
    i = jax.nn.sigmoid(jnp.einsum('bshi,hij->bshj', xh, w_x.astype(jnp.float32)).reshape(B, S, D_RNN) + b_x)
    log_a = -LRU_C * r * jax.nn.softplus(-lam.astype(jnp.float32))
    a = jnp.exp(log_a)
    u = xf * i * jnp.sqrt(-jnp.expm1(2.0 * log_a))
    return linear_scan(a, u, reverse)

def gla_chunked(q, k, v, log_a):
    B, S, H, DK = q.shape
    DV = v.shape[-1]
    N = S // GLA_CHUNK
    q = q.astype(jnp.float32).reshape(B, N, GLA_CHUNK, H, DK)
    k = k.astype(jnp.float32).reshape(B, N, GLA_CHUNK, H, DK)
    v = v.astype(jnp.float32).reshape(B, N, GLA_CHUNK, H, DV)
    b = jnp.cumsum(log_a.astype(jnp.float32).reshape(B, N, GLA_CHUNK, H, DK), axis=2)
    b_last = b[:, :, -1]
    q_e = q * jnp.exp(b)
    k_e = k * jnp.exp(-b)
    scores = jnp.einsum('bnihd,bnjhd->bnhij', q_e, k_e)
    mask = jnp.tril(jnp.ones((GLA_CHUNK, GLA_CHUNK), dtype=bool))
    scores = jnp.where(mask, scores, 0.0)
    o_intra = jnp.einsum('bnhij,bnjhv->bnihv', scores, v)
    k_dec = k * jnp.exp(b_last[:, :, None] - b)
    u = jnp.einsum('bnjhd,bnjhv->bnhdv', k_dec, v)
    decay = jnp.exp(b_last)

    def step(state, inp):
        d, u_n = inp
        return d[..., None] * state + u_n, state

    _, s_prev = lax.scan(step, jnp.zeros((B, H, DK, DV), jnp.float32),
                         (jnp.moveaxis(decay, 1, 0), jnp.moveaxis(u, 1, 0)))
    s_prev = jnp.moveaxis(s_prev, 0, 1)
    o_inter = jnp.einsum('bnihd,bnhdv->bnihv', q_e, s_prev)
    return (o_intra + o_inter).reshape(B, S, H, DV)

def hybrid_mixer(h, w_in, conv_w, conv_b, lru_w_a, lru_b_a, lru_w_x, lru_b_x, lru_lambda,
                 rnn_out_norm, gla_w_gate, gla_b_gate, gla_out_norm, w_out):
    B, S, _ = h.shape
    proj = jnp.einsum('bsd,de->bse', h, w_in)
    p1 = D_RNN
    p2 = p1 + D_RNN
    p3 = p2 + GLA_DK_TOTAL
    p4 = p3 + GLA_DK_TOTAL
    p5 = p4 + GLA_DV_TOTAL
    p6 = p5 + GLA_DV_TOTAL
    p7 = p6 + GLA_RANK
    x_r, gate_r, q, k, v, g, lr_f, lr_b = jnp.split(proj, [p1, p2, p3, p4, p5, p6, p7], axis=-1)

    xc = centred_depthwise_conv(x_r, conv_w, conv_b)
    h_f = rg_lru(xc, lru_w_a[0], lru_b_a[0], lru_w_x[0], lru_b_x[0], lru_lambda[0], False)
    h_b = rg_lru(xc, lru_w_a[1], lru_b_a[1], lru_w_x[1], lru_b_x[1], lru_lambda[1], True)
    y_rnn = (h_f + h_b) * jax.nn.gelu(gate_r.astype(jnp.float32))
    y_rnn = rms_norm(y_rnn, rnn_out_norm).astype(h.dtype)

    qh = q.reshape(B, S, GLA_HEADS, GLA_DK) * (GLA_DK ** -0.5)
    kh = k.reshape(B, S, GLA_HEADS, GLA_DK)
    vh = v.reshape(B, S, GLA_HEADS, GLA_DV)
    la_f = jax.nn.log_sigmoid((jnp.einsum('bsr,re->bse', lr_f, gla_w_gate[0]) + gla_b_gate[0]).astype(jnp.float32)) / GLA_TAU
    la_b = jax.nn.log_sigmoid((jnp.einsum('bsr,re->bse', lr_b, gla_w_gate[1]) + gla_b_gate[1]).astype(jnp.float32)) / GLA_TAU
    la_f = la_f.reshape(B, S, GLA_HEADS, GLA_DK)
    la_b = la_b.reshape(B, S, GLA_HEADS, GLA_DK)
    o_f = gla_chunked(qh, kh, vh, la_f)
    o_b = jnp.flip(gla_chunked(jnp.flip(qh, 1), jnp.flip(kh, 1), jnp.flip(vh, 1), jnp.flip(la_b, 1)), 1)
    o = rms_norm(o_f + o_b, gla_out_norm)
    o = o * jax.nn.silu(g.astype(jnp.float32).reshape(B, S, GLA_HEADS, GLA_DV))
    y_gla = o.reshape(B, S, GLA_DV_TOTAL).astype(h.dtype)

    y = jnp.concatenate([y_rnn, y_gla], axis=-1)
    return jnp.einsum('bse,ed->bsd', y, w_out)

def swiglu(h, w_gate, w_up, w_down):
    a = jnp.einsum('bsd,df->bsf', h, w_gate)
    u = jnp.einsum('bsd,df->bsf', h, w_up)
    return jnp.einsum('bsf,fd->bsd', jax.nn.silu(a) * u, w_down)

def setup_inputs(seed: int = 0) -> dict:
    key = jax.random.key(seed)
    ks = jax.random.split(key, 24)
    L = DEPTH

    def nrm(k, shape, scale):
        return jax.random.normal(k, shape, jnp.float32) * scale

    def gain(k, shape):
        return 1.0 + nrm(k, shape, 0.02)

    u = jax.random.uniform(ks[10], (L, 2, D_RNN), jnp.float32, minval=0.9, maxval=0.999)
    a = u ** (1.0 / LRU_C)
    lam = jnp.log(a) - jnp.log1p(-a)
    return {
        'x': nrm(ks[0], (BATCH, SEQ, D_MODEL), 1.0),
        'mix_norm_pre': gain(ks[1], (L, D_MODEL)),
        'mix_norm_post': gain(ks[2], (L, D_MODEL)),
        'w_in': nrm(ks[3], (L, D_MODEL, D_IN), D_MODEL ** -0.5),
        'conv_w': nrm(ks[4], (L, CONV_WIDTH, D_RNN), CONV_WIDTH ** -0.5),
        'conv_b': nrm(ks[5], (L, D_RNN), 0.01),
        'lru_w_a': nrm(ks[6], (L, 2, RNN_HEADS, RNN_BLOCK, RNN_BLOCK), RNN_BLOCK ** -0.5),
        'lru_b_a': nrm(ks[7], (L, 2, D_RNN), 0.01),
        'lru_w_x': nrm(ks[8], (L, 2, RNN_HEADS, RNN_BLOCK, RNN_BLOCK), RNN_BLOCK ** -0.5),
        'lru_b_x': nrm(ks[9], (L, 2, D_RNN), 0.01),
        'lru_lambda': lam,
        'rnn_out_norm': gain(ks[11], (L, D_RNN)),
        'gla_w_gate': nrm(ks[12], (L, 2, GLA_RANK, GLA_DK_TOTAL), GLA_RANK ** -0.5),
        'gla_b_gate': nrm(ks[13], (L, 2, GLA_DK_TOTAL), 0.1),
        'gla_out_norm': gain(ks[14], (L, GLA_DV)),
        'w_out': nrm(ks[15], (L, D_MIX, D_MODEL), D_MIX ** -0.5),
        'ffn_norm_pre': gain(ks[16], (L, D_MODEL)),
        'ffn_norm_post': gain(ks[17], (L, D_MODEL)),
        'w_ffn_gate': nrm(ks[18], (L, D_MODEL, D_FF), D_MODEL ** -0.5),
        'w_ffn_up': nrm(ks[19], (L, D_MODEL, D_FF), D_MODEL ** -0.5),
        'w_ffn_down': nrm(ks[20], (L, D_FF, D_MODEL), D_FF ** -0.5),
    }

def reference(x, mix_norm_pre, mix_norm_post, w_in, conv_w, conv_b, lru_w_a, lru_b_a,
              lru_w_x, lru_b_x, lru_lambda, rnn_out_norm, gla_w_gate, gla_b_gate,
              gla_out_norm, w_out, ffn_norm_pre, ffn_norm_post, w_ffn_gate, w_ffn_up,
              w_ffn_down):
    for l in range(DEPTH):
        h = rms_norm(x, mix_norm_pre[l])
        m = hybrid_mixer(h, w_in[l], conv_w[l], conv_b[l], lru_w_a[l], lru_b_a[l],
                         lru_w_x[l], lru_b_x[l], lru_lambda[l], rnn_out_norm[l],
                         gla_w_gate[l], gla_b_gate[l], gla_out_norm[l], w_out[l])
        x = x + rms_norm(m, mix_norm_post[l])
        h = rms_norm(x, ffn_norm_pre[l])
        f = swiglu(h, w_ffn_gate[l], w_ffn_up[l], w_ffn_down[l])
        x = x + rms_norm(f, ffn_norm_post[l])
    return x


_drawn_inputs = setup_inputs


def setup_inputs(seed=0):
    import zlib

    import numpy as np

    out = dict(_drawn_inputs(seed))
    spreads = {}
    factors = {'lru_b_a': 28.504,
     'lru_b_x': 8.0,
     'rnn_out_norm': 8.666,
     'gla_out_norm': 14.314,
     'ffn_norm_post': 3.333}
    for name, (base, spread) in spreads.items():
        noise = np.random.default_rng([zlib.crc32(name.encode()), seed]).standard_normal(out[name].shape)
        drawn = base * np.exp(spread * noise) if base else spread * noise
        out[name] = __import__('jax').numpy.asarray(drawn.astype(out[name].dtype))
    for name, factor in factors.items():
        out[name] = (out[name] * factor).astype(out[name].dtype)
    return out
```

```python
from contextlib import ExitStack

import concourse.bass as bass
from concourse import mybir

ALU = mybir.AluOpType
ACT = mybir.ActivationFunctionType
F32 = mybir.dt.float32
F32R = mybir.dt.float32r
U8 = mybir.dt.uint8

P = 128
EPS = 1e-6
LRU_C = 8.0
TAU = 16.0
CHUNK = 64


class Signal:

    def __init__(self, sem, per_layer, before=0):
        self.sem, self.per_layer, self.before = sem, per_layer, before

    def after(self, layer, n):
        return layer * self.per_layer + (n + self.before)


def trunk(nc, x, mix_norm_pre, mix_norm_post, w_in, conv_w, conv_b, lru_w_a, lru_b_a, lru_w_x,
          lru_b_x, lru_lambda, rnn_out_norm, gla_w_gate, gla_b_gate, gla_out_norm, w_out,
          ffn_norm_pre, ffn_norm_post, w_ffn_gate, w_ffn_up, w_ffn_down, out):
    LAYERS, D, D_IN = w_in.shape
    SEQ = x.shape[1]
    D_FF = w_ffn_gate.shape[2]
    D_RNN = conv_w.shape[2]
    RANK, DK_ALL = gla_w_gate.shape[2:]
    DV = gla_out_norm.shape[1]
    HEADS = (D - D_RNN) // DV
    DK = DK_ALL // HEADS
    assert (x.shape[0], SEQ, D, D_RNN, DK, DV, RANK) == (1, 512, 1024, 512, 64, 128, 16)
    NC = D // P
    NS = SEQ // P
    NR = D_RNN // P
    NF = D_FF // P
    PAIRS = HEADS // 2
    NDP = 2 * PAIRS
    NCH = SEQ // CHUNK

    q0 = 2 * D_RNN
    v0 = q0 + 2 * DK_ALL
    g0 = v0 + HEADS * DV
    XR, LR, QK, V, G, GR = 0, NR, NR + 1, NR + 5, NR + 9, NR + 13
    IN_COLS = [c * P for c in range(NR)] + [D_IN - P] + [q0 + c * P for c in range(4)] \
        + [v0 + c * P for c in range(HEADS)] + [g0 + c * P for c in range(HEADS)] \
        + [D_RNN + c * P for c in range(NR)]
    B_OUT = len(IN_COLS)
    B_FF = B_OUT + NC
    B_DOWN = B_FF + 2 * NF
    DOWN_UNITS = [8, 8, NF - 16]
    NB = B_DOWN + 3 * NC
    RAW, SPL = 4, 2
    assert B_OUT % RAW == 1 and NC % RAW == 0 and (2 * NF) % RAW == 0 and (3 * NC) % RAW == 0
    LOADS = [(NB - 1) // RAW + (s == 0) for s in range(RAW)]

    def slot(b, ring):
        return (b if b < B_OUT else b + RAW - 1) % ring

    def loads_before(b):
        return b // RAW if b < B_OUT else (b + RAW - 1) // RAW - (slot(b, RAW) != 0)

    def free_after(b, ring):
        return b - ring + 1 + (ring - 1 if b == B_OUT else 0)

    rows = {}
    n_rows = 0
    for name, n in (("mix_pre", NC), ("mix_post", NC), ("ffn_pre", NC), ("ffn_post", NC),
                    ("conv_w", 4 * NR), ("conv_b", NR), ("b_a", 2 * NR), ("b_x", 2 * NR),
                    ("lam", 2 * NR), ("rnn_norm", NR), ("gla_b", NDP), ("gla_norm", 1)):
        rows[name] = n_rows
        n_rows += n
    COL_TANH = n_rows
    COL_EXP = n_rows + 2 * NR
    n_cols = n_rows + 4 * NR

    ctx = ExitStack()
    with ctx:
        def sb(name, shape, dt=F32, stack=ctx):
            return stack.enter_context(nc.sbuf_tensor(name, shape, dt))

        def sem(name):
            return ctx.enter_context(nc.semaphore(name))

        def signal(name, per_layer, before=0):
            return Signal(sem(name), per_layer, before)

        xT = sb("xT", [P, NC, SEQ])
        h_hi = sb("h_hi", [P, NC, SEQ], F32R)
        h_lo = sb("h_lo", [P, NC, SEQ], F32R)
        raw = sb("raw", [P, RAW, 8 * P])
        w_hi = sb("w_hi", [P, SPL, 8 * P], F32R)
        w_lo = sb("w_lo", [P, SPL, 8 * P], F32R)
        sq = sb("sq", [P, 2, SEQ])
        y32 = sb("y32", [P, 2, SEQ])
        carrier = sb("carrier", [P, 2 * HEADS])
        started = sb("started", [P, 1])
        begun = sb("begun", [P, 4])
        rstd = sb("rstd", [P, SEQ])
        reset = sb("reset", [P, SEQ])
        gla_w = sb("gla_w", [P, 2, DK_ALL])
        ident = sb("ident", [P, P])
        ones = sb("ones", [P, P])
        mask = sb("mask", [P, 2, NS, P], U8)
        prow = sb("prow", [n_rows, LAYERS, P])
        pcol = sb("pcol", [P, LAYERS, n_cols])
        par = sb("par", [P, n_cols])
        decay = sb("decay", [P, NDP, NCH])
        sp = sb("sp", [P, 8, LAYERS, 2 * NR])

        with ExitStack() as region:
            mix = sb("mix", [P, 2 * NF + NC, SEQ], F32, region)
        g_hi = sb("g_hi", [P, NF, SEQ], F32R)
        g_lo = sb("g_lo", [P, NF, SEQ], F32R)
        m = sb("m", [P, NC, SEQ])

        def at(first, n):
            return mix[:, first:first + n, :]

        rnn_r, rnn_i, rnn_t = at(0, 8), at(8, 8), at(16, 8)
        states = at(0, 7).rearrange("p t s -> p (t s)").rearrange(
            "p (k j v) -> p k j v", k=NDP, j=NCH - 1)
        kdT = at(16, 4).rearrange("p k (t d) -> p k t d", t=NS)
        scores = at(20, 4)
        xc = at(24, 4)
        y_rnn = xc
        qk = at(28, 4)
        gate_r = qk
        ke = at(32, 4)
        vT = ke
        lr = mix[96:P, 32, :]
        qe = at(36, 4)
        kdec = at(40, 4)
        v = at(44, 4)
        lru_w = at(44, 4).rearrange("p t s -> p (t s)").rearrange(
            "p (g r t j) -> p g r t j", g=2, r=2, t=NR)
        sg = at(48, 4)
        xs = at(0, 8).rearrange("p t s -> p (t s)").rearrange("p (t d) -> p t d", t=NS)
        mask32 = at(8, 2)

        bank = [ctx.enter_context(nc.psum_tensor(f"bank{i}", [P, SEQ], F32)) for i in range(8)]
        PROJ = [0, 1]
        LRU_BANKS = [2, 3, 4, 5]
        T_BANKS = [6, 2, 3, 4]
        U_BANKS = [[2, 3], [4, 5]]
        S_BANKS = [0, 1]
        O_BANKS = [6, 2]
        DOWN_BANKS = [4, 5]
        STAT = 7

        loaded = [Signal(sem(f"loaded{s}"), 16 * LOADS[s]) for s in range(RAW)]
        hi_made = signal("hi_made", NB)
        lo_made = signal("lo_made", NB, RAW)
        block_used = signal("block_used", NB, SPL)
        s_par, s_x, s_out = sem("s_par"), sem("s_x"), sem("s_out")
        lru_loaded, gla_loaded = signal("lru_loaded", 4 * 16), signal("gla_loaded", 2 * 16)
        const_made, masks_made = sem("const_made"), sem("masks_made")
        par_turned, pcol_made, sp_step, sp_exp = (
            sem("par_turned"), sem("pcol_made"), sem("sp_step"), sem("sp_exp"))
        x_turned, y_turned, y_rows = sem("x_turned"), sem("y_turned"), sem("y_rows")
        par_made, lru_zeroed, scores_zeroed = (
            signal(n, 1) for n in ("par_made", "lru_zeroed", "scores_zeroed"))
        x_made = signal("x_made", 2 * NC, NC)
        SQ_RNN, SQ_HEAD, SQ_POST, SQ_PRE1, SQ_POST1, N_SQ = 8, 12, 16, 24, 32, 40
        sq_made = signal("sq_made", N_SQ)
        ST_RNN, ST_HEAD, ST_POST, ST_PRE1, ST_POST1, N_ST = 8, 12, 16, 17, 25, 26
        stat_mm = signal("stat_mm", N_ST)
        stat_read, rstd_made = signal("stat_read", 9, 1), signal("rstd_made", 9)
        y32_made, y_hi, y_lo = signal("y32_made", 24), signal("y_hi", 24), signal("y_lo", 24)
        head_scaled = signal("head_scaled", HEADS)
        m_made, m_scaled, acc_made = signal("m_made", 16, 2), signal("m_scaled", 16), signal("acc_made", 16)
        silu_made, g32_made = signal("silu_made", NF), signal("g32_made", NF, 1)
        ghi_made, glo_made = signal("ghi_made", NF), signal("glo_made", NF)
        conv_step, lr_made, in_copied = signal("conv_step", 4 * NR), signal("lr_made", 1), signal("in_copied", 16)
        lru_mm, lru_sig, tanh_made = signal("lru_mm", 16), signal("lru_sig", 16), signal("tanh_made", 8)
        z_mm, z_abs, z_min, z_exp, z_log = (
            signal(n, NDP, 1) for n in ("z_mm", "z_abs", "z_min", "z_exp", "z_log"))
        r_exp = signal("r_exp", 8)
        la_made, b_made = signal("la_made", NDP), signal("b_made", NDP)
        eb_made, enb_made = signal("eb_made", NDP), signal("enb_made", NDP)
        decay_made, qe_made, ke_made, kdec_made = (
            signal(n, NDP) for n in ("decay_made", "qe_made", "ke_made", "kdec_made"))
        v_turned, v_made, kd_turned, kd_made = (
            signal(n, 4) for n in ("v_turned", "v_made", "kd_turned", "kd_made"))
        rnn_q, rnn_xi, rnn_a, root_made, rnn_beta, rnn_u = (
            signal(n, 2) for n in ("rnn_q", "rnn_xi", "rnn_a", "root_made", "rnn_beta", "rnn_u"))
        scan_made = signal("scan_made", 8)
        hsum_made, yrnn_made, sgate_made, gelu_made = (
            signal(n, 1) for n in ("hsum_made", "yrnn_made", "sgate_made", "gelu_made"))
        U_GROUPS = [range(0, 4), range(4, NCH - 1)]
        u_mm, state_made = signal("u_mm", NDP * 2), signal("state_made", NDP * (NCH - 1) * 2)
        score_mm, score_kept, o_mm = signal("score_mm", 8), signal("score_kept", 8), signal("o_mm", HEADS)

        def chunk_of(d, j):
            return j if d == 0 else NCH - 1 - j

        block = ctx.enter_context(nc.Block())

        @block.sync
        def _(sp_eng):

            def load_block(l, b, s, src, units=8):
                gap = free_after(b, RAW) if isinstance(b, int) else b + (1 - RAW)
                sp_eng.wait_ge(lo_made.sem, lo_made.after(l, gap))
                sp_eng.dma_start(raw[:, s, 0:units * P].rearrange("p (k c) -> p k c", k=units),
                                 src).then_inc(loaded[s].sem, 16)

            def cols(w, l, c):
                return w[l, :, bass.ds(c, P)].rearrange("(k p) c -> p k c", p=P)

            sp_eng.dma_start(xs, x[0].rearrange("(t p) d -> p t d", p=P)).then_inc(s_x, 16)
            for name, src in (("mix_pre", mix_norm_pre), ("mix_post", mix_norm_post),
                              ("ffn_pre", ffn_norm_pre), ("ffn_post", ffn_norm_post),
                              ("conv_b", conv_b), ("rnn_norm", rnn_out_norm), ("gla_norm", gla_out_norm)):
                n = src.shape[1] // P
                sp_eng.dma_start(prow[rows[name]:rows[name] + n, :, :],
                                 src.rearrange("l (t p) -> t l p", p=P)).then_inc(s_par, 16)
            for name, src in (("conv_w", conv_w), ("b_a", lru_b_a), ("b_x", lru_b_x),
                              ("lam", lru_lambda), ("gla_b", gla_b_gate)):
                n = src.shape[1] * src.shape[2] // P
                sp_eng.dma_start(prow[rows[name]:rows[name] + n, :, :],
                                 src.rearrange("l w (t p) -> (w t) l p", p=P)).then_inc(s_par, 16)

            with sp_eng.Fori(0, LAYERS) as l:
                for b in range(RAW):
                    load_block(l, b, slot(b, RAW), cols(w_in, l, IN_COLS[b]))
                sp_eng.wait_ge(lru_zeroed.sem, lru_zeroed.after(l, 1))
                for g, w in enumerate((lru_w_a, lru_w_x)):
                    for odd in range(2):
                        src = w[l].rearrange("r (t q) i j -> q i (r t) j", q=2)[odd]
                        dst = lru_w.rearrange("p g r t j -> p g (r t) j")
                        sp_eng.dma_start(dst[64 * odd:64 * odd + 64, g, :, 64 * odd:64 * odd + 64],
                                         src).then_inc(lru_loaded.sem, 16)
                sp_eng.wait_ge(z_mm.sem, z_mm.after(l, 0))
                sp_eng.wait_ge(const_made, 3)
                for d in range(2):
                    sp_eng.dma_start(gla_w[96 + RANK * d:96 + RANK * (d + 1), d, :],
                                     gla_w_gate[l, d]).then_inc(gla_loaded.sem, 16)
                for b in range(RAW, B_OUT):
                    load_block(l, b, slot(b, RAW), cols(w_in, l, IN_COLS[b]))
                for c in range(NC):
                    load_block(l, B_OUT + c, slot(B_OUT + c, RAW), cols(w_out, l, c * P))
                with sp_eng.Fori(0, NF // 2) as i:
                    for j in range(2):
                        load_block(l, i * 4 + (B_FF + 2 * j), 2 * j, cols(w_ffn_gate, l, i * (2 * P) + j * P))
                        load_block(l, i * 4 + (B_FF + 2 * j + 1), 2 * j + 1, cols(w_ffn_up, l, i * (2 * P) + j * P))
                for c in range(NC):
                    k = 0
                    for j, units in enumerate(DOWN_UNITS):
                        b = B_DOWN + 3 * c + j
                        load_block(l, b, slot(b, RAW), w_ffn_down[l, k * P:(k + units) * P, bass.ds(c * P, P)]
                                   .rearrange("(k p) c -> p k c", p=P), units)
                        k += units

            for t in range(NS):
                sp_eng.wait_ge(y_rows, 2 * t + 2)
                sp_eng.dma_start(out[0, t * P:(t + 1) * P, :], xs[:, t, :]).then_inc(s_out, 16)
            sp_eng.wait_ge(s_out, 16 * NS)

        @block.gpsimd
        def _(pool):
            pool.memset(ones[:], 1.0).then_inc(const_made, 1)
            pool.memset(ident[:], 0.0).then_inc(const_made, 1)
            pool.memset(gla_w[:], 0.0).then_inc(const_made, 1)
            pool.memset(reset[:], 1.0).then_inc(const_made, 1)
            pool.memset(mask32, 1.0).then_inc(const_made, 1)
            pool.wait_ge(const_made, 5)
            pool.affine_select(out=ident[:], in_=ident[:], compare_op=ALU.not_equal, fill=1.0, base=0,
                               pattern=[[-1, P]], channel_multiplier=1).then_inc(const_made, 1)
            pool.memset(reset[:].rearrange("p (n t) -> p n t", t=CHUNK)[:, :, 0:1], 0.0).then_inc(const_made, 1)
            for d in range(2):
                mv = mask32[:, d, :].rearrange("p (t i) -> p t i", t=NS)
                pool.affine_select(out=mv, in_=mv, compare_op=ALU.is_ge, fill=0.0, base=0,
                                   pattern=[[0, NS], [1 - 2 * d, P]],
                                   channel_multiplier=2 * d - 1).then_inc(const_made, 1)
            pool.wait_ge(const_made, 9)
            for d in range(2):
                mv = mask32[:, d, :].rearrange("p (t i) -> p t i", t=NS)
                pool.memset(mv[64 * d:64 * d + 64, :, 64 * (1 - d):64 * (1 - d) + 64], 0.0).then_inc(const_made, 1)
            pool.wait_ge(const_made, 11)
            pool.memset(started[:], 0.0).then_inc(lo_made.sem, RAW)

            def rest(l, b, b_slot, s, units=8):
                pool.wait_ge(hi_made.sem, hi_made.after(l, b + 1))
                pool.wait_ge(block_used.sem, block_used.after(l, b_slot))
                pool.tensor_tensor(w_lo[:, s % SPL, 0:units * P], raw[:, s, 0:units * P],
                                   w_hi[:, s % SPL, 0:units * P].bitcast(F32),
                                   ALU.subtract).then_inc(lo_made.sem, 1)

            def rest_of(l, b, units=8):
                rest(l, b, free_after(b, SPL), slot(b, RAW), units)

            with pool.Fori(0, LAYERS) as l:
                rest_of(l, 0)
                rest_of(l, 1)
                for b in range(2, B_OUT):
                    rest_of(l, b)
                for c in range(NC):
                    rest_of(l, B_OUT + c)
                with pool.Fori(0, NF // 2) as i:
                    for j in range(4):
                        b = i * 4 + (B_FF + j)
                        rest(l, b, b + (1 - SPL), j)
                for b in range(B_DOWN, NB):
                    rest_of(l, b, DOWN_UNITS[(b - B_DOWN) % 3])

        @block.scalar
        def _(act):
            def head(l, b, s, n_loads, gap, units=8):
                act.wait_ge(loaded[s].sem, loaded[s].after(l, 0) + 16 * (n_loads + 1)
                            if isinstance(n_loads, int) else loaded[s].after(l, 16) + n_loads * 16)
                act.wait_ge(block_used.sem, block_used.after(l, gap))
                act.activation(w_hi[:, s % SPL, 0:units * P], raw[:, s, 0:units * P],
                               ACT.Copy).then_inc(hi_made.sem, 1)

            def head_of(l, b, units=8):
                head(l, b, slot(b, RAW), loads_before(b), free_after(b, SPL), units)

            def inverse_rms(l, n, mms, features):
                act.wait_ge(stat_mm.sem, stat_mm.after(l, mms))
                act.activation(rstd[:], bank[STAT][:], ACT.Ln, bias=EPS, scale=1.0 / features) \
                    .then_inc(stat_read.sem, 1)
                act.wait_ge(stat_read.sem, stat_read.after(l, n + 1))
                act.activation(rstd[:], rstd[:], ACT.Exp, scale=-0.5).then_inc(rstd_made.sem, 1)

            def squares_of_x(l, first, n_sq, n_st):
                for c in range(NC):
                    act.wait_ge(x_made.sem, x_made.after(l, first + c + 1))
                    if c >= 2:
                        act.wait_ge(stat_mm.sem, stat_mm.after(l, n_st + c - 1))
                    act.activation(sq[:, c % 2, :], xT[:, c, :], ACT.Square).then_inc(sq_made.sem, 1)

            def split_hi(l, c, n):
                act.wait_ge(y32_made.sem, y32_made.after(l, n + 1))
                act.activation(h_hi[:, c, :], y32[:, c % 2, :], ACT.Copy).then_inc(y_hi.sem, 1)

            def copy_in(l, b, dst):
                act.wait_ge(block_used.sem, block_used.after(l, b + 1))
                act.activation(dst, bank[PROJ[b % 2]][:], ACT.Copy).then_inc(in_copied.sem, 1)

            def square_of_output(l, c, n_acc):
                act.wait_ge(m_made.sem, m_made.after(l, n_acc + c + 1))
                if c >= 2:
                    act.wait_ge(acc_made.sem, acc_made.after(l, n_acc + c - 1))
                act.activation(sq[:, c % 2, :], m[:, c, :], ACT.Square).then_inc(sq_made.sem, 1)

            act.wait_ge(const_made, 1)
            for n, signalled in enumerate((stat_read, z_abs, z_exp, z_log)):
                act.activation(begun[:, n:n + 1], ones[:, 0:1], ACT.Copy).then_inc(signalled.sem, 1)
            act.wait_ge(pcol_made, LAYERS)
            act.activation(sp[:, 0], pcol[:, :, rows["lam"]:rows["lam"] + 2 * NR], ACT.Abs).then_inc(sp_exp, 1)
            act.wait_ge(sp_exp, 1)
            act.activation(sp[:, 1], sp[:, 0], ACT.Exp, scale=-1.0).then_inc(sp_exp, 1)

            with act.Fori(0, LAYERS) as l:
                head_of(l, 0)
                head_of(l, 1)
                squares_of_x(l, -NC, 0, 0)
                inverse_rms(l, 0, NC, D)
                for c in range(NC):
                    split_hi(l, c, c)

                for b in range(2, QK + 2):
                    head_of(l, b)
                for c in range(4):
                    head_of(l, QK + c + 2)
                    copy_in(l, QK + c, qk[:, c, :])

                act.wait_ge(par_made.sem, par_made.after(l, 1))
                for c in range(NR):
                    for d in range(2):
                        for g, (dst, col) in enumerate(((rnn_r, "b_a"), (rnn_i, "b_x"))):
                            n = 4 * c + 2 * d + g
                            act.wait_ge(lru_mm.sem, lru_mm.after(l, n + 1))
                            k = rows[col] + d * NR + c
                            act.activation(dst[:, d * NR + c, :], bank[LRU_BANKS[2 * d + g]][:], ACT.Sigmoid,
                                           bias=par[:, k:k + 1]).then_inc(lru_sig.sem, 1)
                act.wait_ge(lru_sig.sem, lru_sig.after(l, 16))
                for n in range(2 * NR):
                    act.activation(rnn_t[:, n, :], rnn_r[:, n, :], ACT.Tanh,
                                   scale=par[:, COL_TANH + n:COL_TANH + n + 1]).then_inc(tanh_made.sem, 1)
                head_of(l, V + 2)
                copy_in(l, V, vT[:, 0, :])

                for k in range(NDP):
                    act.wait_ge(z_min.sem, z_min.after(l, k + 1))
                    act.activation(qe[:, k, :], bank[T_BANKS[k]][:], ACT.Abs,
                                   bias=par[:, rows["gla_b"] + k:rows["gla_b"] + k + 1]).then_inc(z_abs.sem, 1)
                act.wait_ge(z_abs.sem, z_abs.after(l, NDP))
                act.activation(qe, qe, ACT.Exp, scale=-1.0).then_inc(z_exp.sem, NDP)
                head_of(l, V + 3)
                copy_in(l, V + 1, vT[:, 1, :])
                act.wait_ge(z_exp.sem, z_exp.after(l, NDP))
                act.activation(qe, qe, ACT.Ln, bias=1.0).then_inc(z_log.sem, NDP)
                act.wait_ge(tanh_made.sem, tanh_made.after(l, 8))
                for n in range(NR):
                    act.activation(rnn_r[:, n, :], rnn_r[:, n, :], ACT.Exp,
                                   scale=par[:, COL_EXP + n:COL_EXP + n + 1]).then_inc(r_exp.sem, 1)
                head_of(l, V + 4)
                copy_in(l, V + 2, vT[:, 2, :])
                for n in range(NR, 2 * NR):
                    act.activation(rnn_r[:, n, :], rnn_r[:, n, :], ACT.Exp,
                                   scale=par[:, COL_EXP + n:COL_EXP + n + 1]).then_inc(r_exp.sem, 1)
                head_of(l, V + 5)
                copy_in(l, V + 3, vT[:, 3, :])

                for k in range(NDP):
                    act.wait_ge(b_made.sem, b_made.after(l, k + 1))
                    act.activation(qe[:, k, :], kdec[:, k, :], ACT.Exp, scale=1.0 / TAU).then_inc(eb_made.sem, 1)
                    if k == 0:
                        act.wait_ge(v_turned.sem, v_turned.after(l, 4))
                    act.activation(ke[:, k, :], kdec[:, k, :], ACT.Exp, scale=-1.0 / TAU).then_inc(enb_made.sem, 1)
                    if k == 1:
                        head_of(l, G + 2)
                        copy_in(l, G, sg[:, 0, :])
                head_of(l, G + 3)
                copy_in(l, G + 1, sg[:, 1, :])
                for d in range(2):
                    act.wait_ge(rnn_q.sem, rnn_q.after(l, d + 1))
                    act.activation(rnn_t[:, d * NR:(d + 1) * NR, :], rnn_t[:, d * NR:(d + 1) * NR, :],
                                   ACT.Sqrt).then_inc(root_made.sem, 1)
                    head_of(l, G + 4 + d)
                    copy_in(l, G + 2 + d, sg[:, 2 + d, :])
                act.wait_ge(in_copied.sem, in_copied.after(l, 12))
                act.activation(sg, sg, ACT.Silu).then_inc(sgate_made.sem, 1)
                act.wait_ge(ke_made.sem, ke_made.after(l, NDP))
                head_of(l, GR + 2)
                copy_in(l, GR, gate_r[:, 0, :])
                head_of(l, GR + 3)
                copy_in(l, GR + 1, gate_r[:, 1, :])
                copy_in(l, GR + 2, gate_r[:, 2, :])
                copy_in(l, GR + 3, gate_r[:, 3, :])
                act.wait_ge(in_copied.sem, in_copied.after(l, 16))
                act.activation(gate_r, gate_r, ACT.Gelu_apprx_tanh).then_inc(gelu_made.sem, 1)
                head_of(l, B_OUT)
                head_of(l, B_OUT + 1)

                act.wait_ge(yrnn_made.sem, yrnn_made.after(l, 1))
                for c in range(NR):
                    if c >= 2:
                        act.wait_ge(stat_mm.sem, stat_mm.after(l, ST_RNN + c - 1))
                    act.activation(sq[:, c % 2, :], y_rnn[:, c, :], ACT.Square).then_inc(sq_made.sem, 1)
                inverse_rms(l, 1, ST_HEAD, D_RNN)
                for c in range(NR):
                    split_hi(l, c, NC + c)
                for h in range(HEADS):
                    act.wait_ge(o_mm.sem, o_mm.after(l, h + 1))
                    act.activation(sq[:, h % 2, :], bank[O_BANKS[h % 2]][:], ACT.Square).then_inc(sq_made.sem, 1)
                    if h:
                        split_hi(l, NR + h - 1, NC + NR + h - 1)
                    if h:
                        act.wait_ge(head_scaled.sem, head_scaled.after(l, h))
                    else:
                        act.wait_ge(y32_made.sem, y32_made.after(l, NC + NR))
                    inverse_rms(l, 2 + h, ST_HEAD + h + 1, DV)
                split_hi(l, NC - 1, 2 * NC - 1)

                for c in range(NC):
                    head_of(l, B_OUT + c + 2)
                    square_of_output(l, c, 0)
                inverse_rms(l, 6, ST_POST + 1, D)

                squares_of_x(l, 0, SQ_PRE1, ST_PRE1)
                inverse_rms(l, 7, ST_PRE1 + NC, D)
                for c in range(NC):
                    split_hi(l, c, 2 * NC + c)

                with act.Fori(0, NF // 2) as i:
                    for j in range(2):
                        f = i * 2 + j
                        b = i * 4 + (B_FF + 2 * j)
                        n2, n3 = (loads_before(B_FF + 2 * j + n) for n in (2, 3))
                        head(l, b + 2, 2 - 2 * j, i + n2, b + (3 - SPL))
                        act.wait_ge(block_used.sem, block_used.after(l, b + 1))
                        act.wait_ge(g32_made.sem, g32_made.after(l, f + (-1)) if j == 1 else g32_made.after(l, f))
                        act.activation(sq[:, j, :], bank[2 * j][:], ACT.Silu).then_inc(silu_made.sem, 1)
                        head(l, b + 3, 3 - 2 * j, i + n3, b + (4 - SPL))
                        act.wait_ge(g32_made.sem, g32_made.after(l, f + 1))
                        act.activation(g_hi[:, bass.ds(f, 1), :], y32[:, j:j + 1, :], ACT.Copy) \
                            .then_inc(ghi_made.sem, 1)
                for c in range(NC):
                    head_of(l, B_DOWN + 3 * c + 2, DOWN_UNITS[2])
                    if c + 1 < NC:
                        head_of(l, B_DOWN + 3 * c + 3)
                        head_of(l, B_DOWN + 3 * c + 4)
                    square_of_output(l, c, NC)
                inverse_rms(l, 8, N_ST, D)

        @block.tensor
        def _(pe):
            def passes(psum, s, unit, a_hi, a_lo, first, last):
                hi, lo = (w[:, s, unit * P:(unit + 1) * P] for w in (w_hi, w_lo))
                pe.matmul(psum, hi, a_hi, start=first, stop=False)
                pe.matmul(psum, hi, a_lo, start=False, stop=False)
                return pe.matmul(psum, lo, a_hi, start=False, stop=last)

            def project(l, b, s, psum, waits=None, n_lo=0):
                pe.wait_ge(lo_made.sem, lo_made.after(l, b + 1))
                for k in range(NC):
                    if waits is not None:
                        pe.wait_ge(y_lo.sem, y_lo.after(l, waits + k + 1))
                    last = passes(bank[psum][:], s, k, h_hi[:, k, :], h_lo[:, k, :], k == 0, k == NC - 1)
                last.then_inc(block_used.sem, 1)

            def stat(l, n_read, src, wait_sem, wait_value, first, last):
                if first:
                    pe.wait_ge(stat_read.sem, stat_read.after(l, n_read))
                pe.wait_ge(wait_sem, wait_value)
                pe.matmul(bank[STAT][:], ones[:], src, start=first, stop=last).then_inc(stat_mm.sem, 1)

            def turn4(dst, srcs, size=P):
                for i, src in enumerate(srcs):
                    last = pe.transpose(dst[:, i * P:(i + 1) * P], src, ident[:])
                return last

            pe.wait_ge(const_made, 6)
            pe.wait_ge(s_par, 16 * 12)
            for l in range(LAYERS):
                pe.transpose(bank[2 + l][:, 0:n_rows], prow[:, l, :], ident[0:n_rows, 0:n_rows]).then_inc(par_turned, 1)
            pe.wait_ge(s_x, 16)
            for c in range(NC):
                if c >= 2:
                    pe.wait_ge(x_made.sem, c - 1)
                for t in range(NS):
                    last = pe.transpose(bank[PROJ[c % 2]][:, t * P:(t + 1) * P], xs[:, t, c * P:(c + 1) * P], ident[:])
                    if c == 0 and t == 0:
                        last.then_inc(block_used.sem, SPL)
                    if c == 0 and t == 1:
                        last.then_inc(z_mm.sem, z_mm.before)
                last.then_inc(x_turned, 1)

            with pe.Fori(0, LAYERS) as l:
                for c in range(NC):
                    stat(l, 0, sq[:, c % 2, :], sq_made.sem, sq_made.after(l, c + 1), c == 0, c == NC - 1)

                def project_in(b, waits=None):
                    project(l, b, slot(b, SPL), PROJ[b % 2], waits)

                project_in(XR, 0)
                project_in(XR + 1)
                for b in range(XR + 2, QK):
                    pe.wait_ge(conv_step.sem, conv_step.after(l, 4 * (b - 1)))
                    project_in(b)
                pe.wait_ge(conv_step.sem, conv_step.after(l, 4 * NR))
                project_in(QK)
                pe.wait_ge(lr_made.sem, lr_made.after(l, 1))
                project_in(QK + 1)
                for b in range(QK + 2, V):
                    pe.wait_ge(in_copied.sem, in_copied.after(l, b - 1 - QK))
                    project_in(b)

                pe.wait_ge(lru_loaded.sem, lru_loaded.after(l, 64))
                for c in range(NR):
                    pe.wait_ge(conv_step.sem, conv_step.after(l, 4 * (c + 1)))
                    for d in range(2):
                        for g in range(2):
                            if c:
                                pe.wait_ge(lru_sig.sem, lru_sig.after(l, 4 * (c - 1) + 2 * d + g + 1))
                            pe.matmul(bank[LRU_BANKS[2 * d + g]][:], lru_w[:, g, d, c, :], xc[:, c, :],
                                      start=True, stop=True).then_inc(lru_mm.sem, 1)
                pe.wait_ge(gla_loaded.sem, gla_loaded.after(l, 32))
                for k in range(NDP):
                    d, pair = divmod(k, PAIRS)
                    if k:
                        pe.wait_ge(lru_sig.sem, lru_sig.after(l, 12 + k))
                    pe.matmul(bank[T_BANKS[k]][:], gla_w[96:P, d, pair * P:(pair + 1) * P], lr,
                              start=True, stop=True).then_inc(z_mm.sem, 1)

                for b in range(V, G):
                    pe.wait_ge(in_copied.sem, in_copied.after(l, b - 1 - QK))
                    project_in(b)
                for c in range(HEADS):
                    pe.wait_ge(in_copied.sem, in_copied.after(l, 8))
                    pe.wait_ge(z_abs.sem, z_abs.after(l, NDP))
                    pe.wait_ge(z_min.sem, z_min.after(l, NDP))
                for t in range(NS):
                    turn4(bank[T_BANKS[t]], [vT[:, c, t * P:(t + 1) * P] for c in range(HEADS)]) \
                        .then_inc(v_turned.sem, 1)
                for b in range(G, GR):
                    pe.wait_ge(in_copied.sem, in_copied.after(l, b - 1 - QK))
                    project_in(b)
                pe.wait_ge(v_made.sem, v_made.after(l, 4))
                for k in range(NDP):
                    pe.wait_ge(kdec_made.sem, kdec_made.after(l, k + 1))
                    turn4(bank[T_BANKS[k]], [kdec[:, k, t * P:(t + 1) * P] for t in range(NS)]) \
                        .then_inc(kd_turned.sem, 1)
                for b in range(GR, B_OUT):
                    pe.wait_ge(in_copied.sem, in_copied.after(l, b - 1 - QK))
                    project_in(b)

                pe.wait_ge(kd_made.sem, kd_made.after(l, 4))
                for k in range(NDP):
                    d, pair = divmod(k, PAIRS)
                    for g, js in enumerate(U_GROUPS):
                        if k:
                            pe.wait_ge(state_made.sem, state_made.after(l, 2 * ((k - 1) * (NCH - 1) + js[-1] + 1)))
                        for j in js:
                            t, half = divmod(chunk_of(d, j), 2)
                            p0, c0 = CHUNK * half, (j - js[0]) // 2 * 2 * DV
                            last = pe.matmul(bank[U_BANKS[g][j % 2]][:, c0:c0 + 2 * DV], kdT[p0:p0 + CHUNK, k, t, :],
                                             v[p0:p0 + CHUNK, t, 2 * pair * DV:2 * (pair + 1) * DV],
                                             start=True, stop=True)
                        last.then_inc(u_mm.sem, 1)

                def score(h):
                    pair, odd = divmod(h, 2)
                    for d in range(2):
                        if h == 0:
                            pe.wait_ge(in_copied.sem, in_copied.after(l, 16))
                        else:
                            pe.wait_ge(score_kept.sem, score_kept.after(l, 2 * (h - 1) + d + 1))
                        for t in range(NS):
                            a, b = (z[DK * odd:DK * odd + DK, d * PAIRS + pair, t * P:(t + 1) * P] for z in (ke, qe))
                            last = pe.matmul(bank[S_BANKS[d]][:, t * P:(t + 1) * P], a, b, start=True, stop=True)
                        last.then_inc(score_mm.sem, 1)

                def output(h):
                    pair, odd = divmod(h, 2)
                    dst = bank[O_BANKS[h % 2]]
                    if h >= 2:
                        pe.wait_ge(head_scaled.sem, head_scaled.after(l, h - 1))
                    for d in range(2):
                        pe.wait_ge(score_kept.sem, score_kept.after(l, 2 * h + d + 1))
                        for t in range(NS):
                            pe.matmul(dst[:, t * P:(t + 1) * P], v[:, t, h * DV:(h + 1) * DV],
                                      scores[:, 2 * d + h % 2, t * P:(t + 1) * P],
                                      start=(d == 0 and t == 0), stop=False, skip_group_check=True)
                    for d in range(2):
                        for j in range(NCH - 1):
                            i0 = chunk_of(d, j + 1) * CHUNK
                            last = pe.matmul(dst[:, i0:i0 + CHUNK],
                                             states[DK * odd:DK * odd + DK, d * PAIRS + pair, j, :],
                                             qe[DK * odd:DK * odd + DK, d * PAIRS + pair, i0:i0 + CHUNK],
                                             start=False, stop=(d == 1 and j == NCH - 2), skip_group_check=True)
                    last.then_inc(o_mm.sem, 1)

                def head_stat(h):
                    stat(l, 2 + h, sq[:, h % 2, :], sq_made.sem, sq_made.after(l, SQ_HEAD + h + 1), True, True)

                score(0)
                for c in range(NR):
                    stat(l, 1, sq[:, c % 2, :], sq_made.sem, sq_made.after(l, SQ_RNN + c + 1), c == 0, c == NR - 1)
                pe.wait_ge(state_made.sem, state_made.after(l, state_made.per_layer))
                for h in range(HEADS):
                    if h + 1 < HEADS:
                        score(h + 1)
                    output(h)
                    if h:
                        head_stat(h - 1)
                head_stat(HEADS - 1)

                with pe.Fori(0, NC // 4) as i:
                    for j in range(4):
                        b = i * 4 + (B_OUT + j)
                        if j < 2:
                            pe.wait_ge(score_kept.sem, score_kept.after(l, 8))
                        pe.wait_ge(m_made.sem, m_made.after(l, i * 4 + (j - 1)))
                        project(l, b, j % SPL, PROJ[j % 2], NC)
                stat(l, 6, y32[:, 0, :], acc_made.sem, acc_made.after(l, NC), True, True)

                for c in range(NC):
                    stat(l, 7, sq[:, c % 2, :], sq_made.sem, sq_made.after(l, SQ_PRE1 + c + 1), c == 0, c == NC - 1)
                with pe.Fori(0, NF // 2) as i:
                    for j in range(2):
                        for u in range(2):
                            pe.wait_ge(g32_made.sem, g32_made.after(l, i * 2))
                            project(l, i * 4 + (B_FF + 2 * j + u), u, 2 * j + u, 2 * NC)
                with pe.Fori(0, NC // 4) as i:
                    for j in range(4):
                        psum = DOWN_BANKS[j % 2]
                        pe.wait_ge(m_made.sem, m_made.after(l, i * 4 + (NC + j - 1)))
                        k = 0
                        for n, units in enumerate(DOWN_UNITS):
                            pe.wait_ge(lo_made.sem, lo_made.after(l, i * 12 + (B_DOWN + 3 * j + n + 1)))
                            if n == 2:
                                pe.wait_ge(glo_made.sem, glo_made.after(l, NF))
                            elif n == 1:
                                pe.wait_ge(glo_made.sem, glo_made.after(l, 16))
                            else:
                                pe.wait_ge(glo_made.sem, glo_made.after(l, 8))
                            for u in range(units):
                                last = passes(bank[psum][:], (3 * j + n) % SPL, u, g_hi[:, k, :], g_lo[:, k, :],
                                              k == 0, k == NF - 1)
                                k += 1
                            last.then_inc(block_used.sem, 1)
                stat(l, 8, y32[:, 0, :], acc_made.sem, acc_made.after(l, 2 * NC), True, True)

            for t in range(NS):
                for half in range(2):
                    n = 2 * t + half
                    pe.wait_ge(x_made.sem, x_made.after(LAYERS, 0))
                    if n >= 2:
                        pe.wait_ge(y_rows, n - 1)
                    turn4(bank[n % 2], [xT[:, 4 * half + i, t * P:(t + 1) * P] for i in range(4)]) \
                        .then_inc(y_turned, 1)

        @block.vector
        def _(dve):
            dve.memset(carrier[:, 0:1], 0.0).then_inc(m_made.sem, 2)
            dve.memset(carrier[:, 1:2], 0.0).then_inc(g32_made.sem, 1)
            dve.memset(carrier[:, 2:3], 0.0).then_inc(z_min.sem, 1)
            dve.wait_ge(const_made, 11)
            dve.tensor_copy(mask[:], mask32.rearrange("p d (t i) -> p d t i", t=NS)).then_inc(masks_made, 1)
            for l in range(LAYERS):
                dve.wait_ge(par_turned, l + 1)
                dve.tensor_copy(pcol[:, l, 0:n_rows], bank[2 + l][:, 0:n_rows]).then_inc(pcol_made, 1)
            for c in range(NC):
                dve.wait_ge(x_turned, c + 1)
                dve.tensor_copy(xT[:, c, :], bank[PROJ[c % 2]][:]).then_inc(x_made.sem, 1)

            done = [0]

            def step(ins):
                done[0] += 1
                ins.then_inc(sp_step, 1)
                dve.wait_ge(sp_step, done[0])

            lam = pcol[:, :, rows["lam"]:rows["lam"] + 2 * NR]
            dve.wait_ge(pcol_made, LAYERS)
            dve.wait_ge(sp_exp, 2)
            step(dve.tensor_scalar(sp[:, 2], sp[:, 1], 2.0, None, ALU.add))
            step(dve.reciprocal(sp[:, 3], sp[:, 2]))
            step(dve.tensor_tensor(sp[:, 4], sp[:, 1], sp[:, 3], ALU.mult))
            step(dve.tensor_tensor(sp[:, 5], sp[:, 4], sp[:, 4], ALU.mult))
            step(dve.tensor_scalar(sp[:, 6], sp[:, 5], 1.0 / 19, None, ALU.mult))
            for odd in range(17, 1, -2):
                step(dve.scalar_tensor_tensor(sp[:, 6], sp[:, 6], 1.0 / odd, sp[:, 5], ALU.add, ALU.mult))
            step(dve.scalar_tensor_tensor(sp[:, 6], sp[:, 6], 1.0, sp[:, 4], ALU.add, ALU.mult))
            step(dve.tensor_scalar(sp[:, 7], lam, -1.0, 0.0, ALU.mult, ALU.max))
            step(dve.scalar_tensor_tensor(sp[:, 7], sp[:, 6], 2.0, sp[:, 7], ALU.mult, ALU.add))
            dve.tensor_scalar(pcol[:, :, COL_TANH:COL_TANH + 2 * NR], sp[:, 7], LRU_C / 2, None,
                              ALU.mult).then_inc(pcol_made, 1)
            dve.tensor_scalar(pcol[:, :, COL_EXP:COL_EXP + 2 * NR], sp[:, 7], -LRU_C, None,
                              ALU.mult).then_inc(pcol_made, 1)
            dve.wait_ge(pcol_made, LAYERS + 2)

            def col(name, k=0):
                k += rows[name]
                return par[:, k:k + 1]

            def split_lo(l, c, n):
                dve.wait_ge(y_hi.sem, y_hi.after(l, n + 1))
                dve.tensor_tensor(h_lo[:, c, :], y32[:, c % 2, :], h_hi[:, c, :].bitcast(F32),
                                  ALU.subtract).then_inc(y_lo.sem, 1)

            def normalise(l, n, chunks, src, gain, n_rstd):
                dve.wait_ge(rstd_made.sem, rstd_made.after(l, n_rstd + 1))
                for c in range(chunks):
                    if c >= 2:
                        dve.wait_ge(y_lo.sem, y_lo.after(l, n + c - 1))
                    dve.scalar_tensor_tensor(y32[:, c % 2, :], src[:, c, :], col(gain, c), rstd[:],
                                             ALU.mult, ALU.mult).then_inc(y32_made.sem, 1)
                    if c:
                        split_lo(l, c - 1, n + c - 1)
                split_lo(l, chunks - 1, n + chunks - 1)

            def take_output(l, c, b, psum, n, n_sq):
                dve.wait_ge(block_used.sem, block_used.after(l, b + 1))
                dve.tensor_copy(m[:, c, :], bank[psum][:]).then_inc(m_made.sem, 1)
                dve.wait_ge(sq_made.sem, sq_made.after(l, n_sq + c + 1))
                if c == 0:
                    dve.tensor_copy(y32[:, 0, :], sq[:, 0, :]).then_inc(acc_made.sem, 1)
                else:
                    dve.wait_ge(acc_made.sem, acc_made.after(l, n + c))
                    dve.tensor_tensor(y32[:, 0, :], y32[:, 0, :], sq[:, c % 2, :], ALU.add).then_inc(acc_made.sem, 1)

            def add_branch(l, n, gain, n_rstd):
                dve.wait_ge(rstd_made.sem, rstd_made.after(l, n_rstd + 1))
                dve.wait_ge(m_made.sem, m_made.after(l, n + NC))
                for c in range(NC + 1):
                    if c < NC:
                        dve.scalar_tensor_tensor(m[:, c, :], m[:, c, :], col(gain, c), rstd[:],
                                                 ALU.mult, ALU.mult).then_inc(m_scaled.sem, 1)
                    if c:
                        dve.wait_ge(m_scaled.sem, m_scaled.after(l, n + c))
                        dve.tensor_tensor(xT[:, c - 1, :], xT[:, c - 1, :], m[:, c - 1, :],
                                          ALU.add).then_inc(x_made.sem, 1)

            with dve.Fori(0, LAYERS) as l:
                dve.tensor_copy(par[:].rearrange("p (o n) -> p o n", o=1), pcol[:, bass.ds(l, 1), :]) \
                    .then_inc(par_made.sem, 1)
                dve.wait_ge(par_made.sem, par_made.after(l, 1))
                dve.wait_ge(x_made.sem, x_made.after(l, 0))
                normalise(l, 0, NC, xT, "mix_pre", 0)

                dve.memset(at(44, 4), 0.0).then_inc(lru_zeroed.sem, 1)

                for c in range(NR):
                    dve.wait_ge(block_used.sem, block_used.after(l, XR + c + 1))
                    psum = bank[PROJ[c % 2]]
                    dve.tensor_scalar(xc[:, c, :], psum[:], col("conv_w", 2 * NR + c), col("conv_b", c),
                                      ALU.mult, ALU.add).then_inc(conv_step.sem, 1)
                    for n, (tap, shift) in enumerate(((0, -2), (1, -1), (3, 1))):
                        lo, hi = max(0, -shift), SEQ - max(0, shift)
                        dve.wait_ge(conv_step.sem, conv_step.after(l, 4 * c + n + 1))
                        dve.scalar_tensor_tensor(xc[:, c, lo:hi], psum[:, lo + shift:hi + shift],
                                                 col("conv_w", tap * NR + c), xc[:, c, lo:hi],
                                                 ALU.mult, ALU.add).then_inc(conv_step.sem, 1)
                dve.wait_ge(block_used.sem, block_used.after(l, LR + 1))
                dve.tensor_copy(lr, bank[PROJ[LR % 2]][96:P, :]).then_inc(lr_made.sem, 1)

                for k in range(NDP):
                    dve.wait_ge(z_mm.sem, z_mm.after(l, k + 1))
                    dve.tensor_scalar(kdec[:, k, :], bank[T_BANKS[k]][:], col("gla_b", k), 0.0,
                                      ALU.add, ALU.min).then_inc(z_min.sem, 1)
                dve.wait_ge(z_log.sem, z_log.after(l, NDP))
                dve.wait_ge(z_min.sem, z_min.after(l, NDP))
                for k in range(NDP):
                    dve.tensor_tensor(kdec[:, k, :], kdec[:, k, :], qe[:, k, :], ALU.subtract) \
                        .then_inc(la_made.sem, 1)
                for k in range(NDP):
                    dve.wait_ge(la_made.sem, la_made.after(l, k + 1))
                    seq = kdec[:, k, :] if k < PAIRS else kdec[:, k, ::-1]
                    dve.tensor_tensor_scan(seq, reset[:], seq, 0.0, ALU.mult, ALU.add).then_inc(b_made.sem, 1)

                def group(z, d):
                    return z[:, d * NR:(d + 1) * NR, :]

                for d in range(2):
                    dve.wait_ge(r_exp.sem, r_exp.after(l, NR * (d + 1)))
                    r, i, t = group(rnn_r, d), group(rnn_i, d), group(rnn_t, d)
                    dve.scalar_tensor_tensor(r, r, 1.0, t, ALU.add, ALU.mult).then_inc(rnn_q.sem, 1)
                    dve.tensor_tensor(i, i, xc, ALU.mult).then_inc(rnn_xi.sem, 1)
                    dve.wait_ge(rnn_q.sem, rnn_q.after(l, d + 1))
                    dve.tensor_scalar(r, r, -1.0, 1.0, ALU.mult, ALU.add).then_inc(rnn_a.sem, 1)

                for t in range(NS):
                    dve.wait_ge(v_turned.sem, v_turned.after(l, t + 1))
                    dve.tensor_copy(v[:, t, :], bank[T_BANKS[t]][:]).then_inc(v_made.sem, 1)

                for k in range(NDP):
                    d, pair = divmod(k, PAIRS)
                    dve.wait_ge(eb_made.sem, eb_made.after(l, k + 1))
                    dve.wait_ge(enb_made.sem, enb_made.after(l, k + 1))
                    last = 0 if d else CHUNK - 1
                    dve.tensor_copy(decay[:, k, :], qe[:, k, :].rearrange("p (n t) -> p n t", t=CHUNK)[:, :, last]) \
                        .then_inc(decay_made.sem, 1)
                    dve.tensor_tensor(ke[:, k, :], qk[:, PAIRS + pair, :], ke[:, k, :], ALU.mult).then_inc(ke_made.sem, 1)
                    dve.wait_ge(decay_made.sem, decay_made.after(l, k + 1))
                    dve.scalar_tensor_tensor(qe[:, k, :], qk[:, pair, :], DK ** -0.5, qe[:, k, :],
                                             ALU.mult, ALU.mult).then_inc(qe_made.sem, 1)
                    dve.wait_ge(ke_made.sem, ke_made.after(l, k + 1))
                    chunks = [z[:, k, :].rearrange("p (n t) -> p n t", t=CHUNK) for z in (kdec, ke)]
                    dve.tensor_tensor(chunks[0], chunks[1],
                                      decay[:, k, :].rearrange("p (n o) -> p n o", o=1).to_broadcast([P, NCH, CHUNK]),
                                      ALU.mult).then_inc(kdec_made.sem, 1)

                for d in range(2):
                    r, i, t = group(rnn_r, d), group(rnn_i, d), group(rnn_t, d)
                    dve.wait_ge(root_made.sem, root_made.after(l, d + 1))
                    dve.wait_ge(rnn_a.sem, rnn_a.after(l, d + 1))
                    dve.scalar_tensor_tensor(t, r, 1.0, t, ALU.add, ALU.mult).then_inc(rnn_beta.sem, 1)
                    dve.wait_ge(rnn_beta.sem, rnn_beta.after(l, d + 1))
                    dve.tensor_tensor(i, i, t, ALU.mult).then_inc(rnn_u.sem, 1)
                    dve.wait_ge(rnn_u.sem, rnn_u.after(l, d + 1))
                    for c in range(NR):
                        a, u = (z[:, d * NR + c, :] if d == 0 else z[:, d * NR + c, ::-1] for z in (rnn_r, rnn_i))
                        dve.tensor_tensor_scan(u, a, u, 0.0, ALU.mult, ALU.add).then_inc(scan_made.sem, 1)
                dve.wait_ge(scan_made.sem, scan_made.after(l, 8))
                dve.tensor_tensor(group(rnn_i, 0), group(rnn_i, 0), group(rnn_i, 1), ALU.add).then_inc(hsum_made.sem, 1)
                for k in range(NDP):
                    dve.wait_ge(kd_turned.sem, kd_turned.after(l, k + 1))
                    dve.tensor_copy(kdT[:, k], bank[T_BANKS[k]][:].rearrange("p (t d) -> p t d", t=NS)) \
                        .then_inc(kd_made.sem, 1)
                dve.memset(scores, 0.0).then_inc(scores_zeroed.sem, 1)
                dve.wait_ge(scores_zeroed.sem, scores_zeroed.after(l, 1))
                dve.wait_ge(gelu_made.sem, gelu_made.after(l, 1))
                dve.wait_ge(hsum_made.sem, hsum_made.after(l, 1))
                dve.tensor_tensor(y_rnn, group(rnn_i, 0), gate_r, ALU.mult).then_inc(yrnn_made.sem, 1)

                for k in range(NDP):
                    d = k // PAIRS
                    for j in range(NCH - 1):
                        g, n = j // 4, (k * (NCH - 1) + j) * 2
                        dve.wait_ge(u_mm.sem, u_mm.after(l, 2 * k + g + 1))
                        if j:
                            dve.wait_ge(state_made.sem, state_made.after(l, n))
                        for odd in range(2):
                            p = slice(DK * odd, DK * odd + DK)
                            c0 = (2 * (j % 4 // 2) + odd) * DV
                            u = bank[U_BANKS[g][j % 2]][p, c0:c0 + DV]
                            c = chunk_of(d, j)
                            if j == 0:
                                last = dve.tensor_copy(states[p, k, j, :], u)
                            else:
                                last = dve.scalar_tensor_tensor(states[p, k, j, :], states[p, k, j - 1, :],
                                                                decay[p, k, c:c + 1], u, ALU.mult, ALU.add)
                            last.then_inc(state_made.sem, 1)


                def keep(h):
                    if h >= 2:
                        dve.wait_ge(o_mm.sem, o_mm.after(l, h - 1))
                    for d in range(2):
                        dve.wait_ge(score_mm.sem, score_mm.after(l, 2 * h + d + 1))
                        dve.tensor_copy(carrier[:, 2 * h + d:2 * h + d + 1], ones[:, 0:1])
                        dve.copy_predicated(scores[:, 2 * d + h % 2, :].rearrange("p (t i) -> p t i", t=NS),
                                            mask[:, d], bank[S_BANKS[d]][:].rearrange("p (t i) -> p t i", t=NS)) \
                            .then_inc(score_kept.sem, 1)

                keep(0)
                dve.wait_ge(block_used.sem, block_used.after(l, B_OUT))
                normalise(l, NC, NR, y_rnn, "rnn_norm", 1)
                keep(1)
                dve.wait_ge(sgate_made.sem, sgate_made.after(l, 1))
                for h in range(HEADS):
                    n = NC + NR + h
                    dve.wait_ge(rstd_made.sem, rstd_made.after(l, 3 + h))
                    dve.wait_ge(y_lo.sem, y_lo.after(l, n - 1))
                    dve.scalar_tensor_tensor(y32[:, h % 2, :], bank[O_BANKS[h % 2]][:], col("gla_norm"), rstd[:],
                                             ALU.mult, ALU.mult).then_inc(head_scaled.sem, 1)
                    dve.wait_ge(head_scaled.sem, head_scaled.after(l, h + 1))
                    dve.tensor_tensor(y32[:, h % 2, :], y32[:, h % 2, :], sg[:, h, :], ALU.mult) \
                        .then_inc(y32_made.sem, 1)
                    if h + 2 < HEADS:
                        keep(h + 2)
                    split_lo(l, NR + h, n)

                for c in range(NC):
                    take_output(l, c, B_OUT + c, PROJ[c % 2], 0, SQ_POST)
                add_branch(l, 0, "mix_post", 6)
                dve.wait_ge(x_made.sem, x_made.after(l, NC))
                normalise(l, 2 * NC, NC, xT, "ffn_pre", 7)

                with dve.Fori(0, NF // 2) as i:
                    for j in range(2):
                        f = i * 2 + j
                        b = i * 4 + (B_FF + 2 * j + 1)
                        dve.wait_ge(block_used.sem, block_used.after(l, b + 1))
                        dve.wait_ge(silu_made.sem, silu_made.after(l, f + 1))
                        dve.tensor_tensor(y32[:, j, :], sq[:, j, :], bank[2 * j + 1][:], ALU.mult) \
                            .then_inc(g32_made.sem, 1)
                        dve.wait_ge(ghi_made.sem, ghi_made.after(l, f + 1))
                        dve.tensor_tensor(g_lo[:, bass.ds(f, 1), :], y32[:, j:j + 1, :],
                                          g_hi[:, bass.ds(f, 1), :].bitcast(F32), ALU.subtract) \
                            .then_inc(glo_made.sem, 1)
                dve.wait_ge(glo_made.sem, glo_made.after(l, NF))
                for c in range(NC):
                    take_output(l, c, B_DOWN + 3 * c + 2, DOWN_BANKS[c % 2], NC, SQ_POST1)
                add_branch(l, NC, "ffn_post", 8)

            for n in range(2 * NS):
                t, half = divmod(n, 2)
                dve.wait_ge(y_turned, n + 1)
                dve.tensor_copy(xs[:, t, half * 512:(half + 1) * 512], bank[n % 2][:]).then_inc(y_rows, 1)


_INS = ['x', 'mix_norm_pre', 'mix_norm_post', 'w_in', 'conv_w', 'conv_b', 'lru_w_a', 'lru_b_a', 'lru_w_x',
        'lru_b_x', 'lru_lambda', 'rnn_out_norm', 'gla_w_gate', 'gla_b_gate', 'gla_out_norm', 'w_out',
        'ffn_norm_pre', 'ffn_norm_post', 'w_ffn_gate', 'w_ffn_up', 'w_ffn_down']


def kernel(**inputs):
    import numpy as np
    import concourse.bacc as bacc
    from concourse.bass_utils import run_bass_kernel_spmd

    nc = bacc.Bacc("TRN2", target_bir_lowering=False, num_devices=1)
    arrays, args = {}, []
    for name in _INS:
        a = np.ascontiguousarray(inputs[name])
        arrays[f"in_{name}"] = a
        args.append(nc.dram_tensor(f"in_{name}", a.shape, mybir.dt.from_np(a.dtype), kind="ExternalInput").ap())
    shape = arrays["in_x"].shape
    args.append(nc.dram_tensor("out_x", shape, F32, kind="ExternalOutput").ap())
    trunk(nc, *args)
    r = run_bass_kernel_spmd(nc, [arrays], core_ids=[0])
    return r.results[0]["out_x"]
```

```python
from contextlib import ExitStack

import concourse.bass as bass
from concourse import mybir

ALU = mybir.AluOpType
ACT = mybir.ActivationFunctionType
F32 = mybir.dt.float32
F32R = mybir.dt.float32r
U8 = mybir.dt.uint8
BF16 = mybir.dt.bfloat16

P = 128
EPS = 1e-6
LRU_C = 8.0
TAU = 16.0
CHUNK = 64

EXP_LN = "natural_log_exp_and_others"
SILU = "silu_and_others"


class Signal:

    def __init__(self, sem, per_layer, before=0):
        self.sem, self.per_layer, self.before = sem, per_layer, before

    def after(self, layer, n):
        return layer * self.per_layer + (n + self.before)


def trunk(nc, x, mix_norm_pre, mix_norm_post, w_in, conv_w, conv_b, lru_w_a, lru_b_a, lru_w_x,
          lru_b_x, lru_lambda, rnn_out_norm, gla_w_gate, gla_b_gate, gla_out_norm, w_out,
          ffn_norm_pre, ffn_norm_post, w_ffn_gate, w_ffn_up, w_ffn_down, out):
    LAYERS, D, D_IN = w_in.shape
    SEQ = x.shape[1]
    D_FF = w_ffn_gate.shape[2]
    D_RNN = conv_w.shape[2]
    RANK, DK_ALL = gla_w_gate.shape[2:]
    DV = gla_out_norm.shape[1]
    HEADS = (D - D_RNN) // DV
    DK = DK_ALL // HEADS
    assert (x.shape[0], SEQ, D, D_RNN, DK, DV, RANK) == (1, 512, 1024, 512, 64, 128, 16)
    NC = D // P
    NS = SEQ // P
    NR = D_RNN // P
    NF = D_FF // P
    PAIRS = HEADS // 2
    NDP = 2 * PAIRS
    NCH = SEQ // CHUNK

    q0 = 2 * D_RNN
    v0 = q0 + 2 * DK_ALL
    g0 = v0 + HEADS * DV
    XR, LR, QK, V, G, GR = 0, NR, NR + 1, NR + 5, NR + 9, NR + 13
    IN_COLS = [c * P for c in range(NR)] + [D_IN - P] + [q0 + c * P for c in range(4)] \
        + [v0 + c * P for c in range(HEADS)] + [g0 + c * P for c in range(HEADS)] \
        + [D_RNN + c * P for c in range(NR)]
    B_OUT = len(IN_COLS)
    B_FF = B_OUT + NC
    B_DOWN = B_FF + 2 * NF
    DOWN_UNITS = [8, 8, NF - 16]
    NB = B_DOWN + 3 * NC
    RAW, SPL = 2, 4
    GAP = SPL - 1
    assert B_OUT % SPL == 1 and NC % SPL == 0 and (2 * NF) % SPL == 0 and (3 * NC) % SPL == 0

    def slot(b, ring):
        return (b if b < B_OUT else b + GAP) % ring

    def loads_before(b):
        return sum(slot(a, RAW) == slot(b, RAW) for a in range(b))

    LOADS = [sum(slot(a, RAW) == s for a in range(NB)) for s in range(RAW)]

    def free_after(b, ring):
        return b if b == B_OUT else b - ring + 1

    rows = {}
    n_rows = 0
    for name, n in (("mix_pre", NC), ("mix_post", NC), ("ffn_pre", NC), ("ffn_post", NC),
                    ("conv_w", 4 * NR), ("conv_b", NR), ("b_a", 2 * NR), ("b_x", 2 * NR),
                    ("lam", 2 * NR), ("rnn_norm", NR), ("gla_b", NDP), ("gla_norm", 1)):
        rows[name] = n_rows
        n_rows += n
    COL_TANH = n_rows
    COL_EXP = n_rows + 2 * NR
    n_cols = n_rows + 4 * NR

    ctx = ExitStack()
    with ctx:
        def sb(name, shape, dt=F32, stack=ctx):
            return stack.enter_context(nc.sbuf_tensor(name, shape, dt))

        def sem(name):
            return ctx.enter_context(nc.semaphore(name))

        def signal(name, per_layer, before=0):
            return Signal(sem(name), per_layer, before)

        xT = sb("xT", [P, NC, SEQ])
        h_hi = sb("h_hi", [P, NC, SEQ], F32R)
        h_lo = sb("h_lo", [P, NC, SEQ], F32R)
        raw = sb("raw", [P, RAW, 8 * P])
        w_hi = sb("w_hi", [P, SPL, 8 * P], F32R)
        w_lo = sb("w_lo", [P, SPL, 8 * P], F32R)
        sq = sb("sq", [P, 2, SEQ])
        y32 = sb("y32", [P, 2, SEQ])
        carrier = sb("carrier", [P, 2 * HEADS])
        started = sb("started", [P, 1])
        begun = sb("begun", [P, 4])
        rstd = sb("rstd", [P, SEQ])
        rstd_h = sb("rstd_h", [P, SEQ])
        reset = sb("reset", [P, SEQ], BF16)
        ident = sb("ident", [P, P])
        ones = sb("ones", [P, P])
        mask = sb("mask", [P, 2, P], U8)
        pcol = sb("pcol", [P, LAYERS, n_cols])
        par = sb("par", [P, n_cols])
        pre_gain = sb("pre_gain", [P, LAYERS + 1, NC])
        next_gain = sb("next_gain", [P, NC])
        decay = sb("decay", [P, NDP, NCH])

        with ExitStack() as region:
            mix = sb("mix", [P, 2 * NF + NC, SEQ], F32, region)
        g_hi = sb("g_hi", [P, NF, SEQ], F32R)
        g_lo = sb("g_lo", [P, NF, SEQ], F32R)
        m = sb("m", [P, NC, SEQ])

        def at(first, n):
            return mix[:, first:first + n, :]

        x_r = at(0, 4)
        rnn_r, rnn_i, rnn_t = at(0, 8), at(8, 8), at(16, 8)
        states = at(0, 7).rearrange("p t s -> p (t s)").rearrange(
            "p (k j v) -> p k j v", k=NDP, j=NCH - 1)
        kdT = at(16, 4).rearrange("p k (t d) -> p k t d", t=NS)
        scores = at(20, 4)
        xc = at(24, 4)
        y_rnn = xc
        qk = at(28, 4)
        gate_r = qk
        ke = at(32, 4)
        vT = ke
        lr, gla_w = mix[96:P, 32, :], mix[96:P, 33, :]
        qe = at(36, 4)
        kdec = at(40, 4)
        v = at(44, 4)
        lru_w = at(44, 4).rearrange("p t s -> p (t s)").rearrange(
            "p (g r t j) -> p g r t j", g=2, r=2, t=NR)
        sg = at(48, 4)
        xs = at(0, 8).rearrange("p t s -> p (t s)").rearrange("p (t d) -> p t d", t=NS)
        mask32 = mix[:, 8, 0:2 * P].rearrange("p (d i) -> p d i", d=2)
        prow = mix[0:n_rows, 9, 0:LAYERS * P].rearrange("r (l p) -> r l p", l=LAYERS)
        sp = mix[:, 10, 0:8 * LAYERS * 2 * NR].rearrange("p (n l k) -> p n l k", n=8, l=LAYERS)

        bank = [ctx.enter_context(nc.psum_tensor(f"bank{i}", [P, SEQ], F32)) for i in range(8)]
        X_BANKS = [4, 5]
        FIRST = [0, 1, 2, 3]
        PROJ = [0, 1]
        LRU_BANKS = [2, 3, 4, 5]
        T_BANKS = [6, 2, 3, 4]
        U_BANKS = [[2, 3], [4, 5]]
        S_BANKS = [[0, 1], [4, 5]]
        O_BANKS = [6, 2, 3, 0]
        OUT_BANKS = [4, 5]
        STAT = 7

        loaded = [Signal(sem(f"loaded{s}"), 16 * LOADS[s]) for s in range(RAW)]
        hi_made = signal("hi_made", NB)
        lo_made = signal("lo_made", NB, RAW)
        block_used = signal("block_used", NB, SPL)
        s_par, s_out = sem("s_par"), sem("s_out")
        s_x = [sem(f"s_x{n}") for n in range(NC // 2)]
        lru_loaded, gla_loaded = signal("lru_loaded", 4 * 16), signal("gla_loaded", 2 * 16)
        const_made, masks_made = sem("const_made"), sem("masks_made")
        par_turned, pcol_made, gain_made, sp_step, sp_exp = (
            sem(n) for n in ("par_turned", "pcol_made", "gain_made", "sp_step", "sp_exp"))
        x_turned, y_turned, y_rows = sem("x_turned"), sem("y_turned"), sem("y_rows")
        par_made, lru_zeroed, scores_zeroed = signal("par_made", 2), signal("lru_zeroed", 2), signal("scores_zeroed", 1)
        x_made = signal("x_made", 2 * NC, NC)
        SQ_RNN, SQ_HEAD, SQ_POST, SQ_POST1, N_SQ = 0, 4, 8, 16, 24
        sq_made = signal("sq_made", N_SQ)
        xsq_made, xacc_made = signal("xsq_made", 2 * NC, NC), signal("xacc_made", 2 * (NC - 1), NC - 1)
        ST_RNN, ST_HEAD, ST_POST, ST_PRE1, ST_POST1, N_ST = 1, 5, 9, 11, 12, 14
        stat_mm = signal("stat_mm", N_ST)
        stat_read, rstd_made = signal("stat_read", 9, 1), signal("rstd_made", 9)
        H_Y, H_X1, H_X2 = 0, NC, 2 * NC
        y32_made, y_hi, y_lo = signal("y32_made", NC), signal("y_hi", 3 * NC, NC), signal("y_lo", 3 * NC, NC)
        head_scaled = signal("head_scaled", HEADS)
        m_made, m_scaled, acc_made = signal("m_made", 16, 2), signal("m_scaled", 16), signal("acc_made", 2 * (NC - 1))
        gate_scaled, silu_made, up_scaled, g32_made = (
            signal(n, NF) for n in ("gate_scaled", "silu_made", "up_scaled", "g32_made"))
        ghi_made, glo_made = signal("ghi_made", NF), signal("glo_made", NF)
        conv_step, in_made = signal("conv_step", 4 * NR), signal("in_made", B_OUT)
        lru_mm, lru_sig, tanh_made = signal("lru_mm", 16), signal("lru_sig", 16), signal("tanh_made", 8)
        z_mm, z_abs, z_min, z_exp, z_log = (
            signal(n, NDP, 1) for n in ("z_mm", "z_abs", "z_min", "z_exp", "z_log"))
        r_exp = signal("r_exp", 8)
        la_made, b_made = signal("la_made", NDP), signal("b_made", NDP)
        eb_made, enb_made = signal("eb_made", NDP), signal("enb_made", NDP)
        decay_made, qe_made, ke_made, kdec_made = (
            signal(n, NDP) for n in ("decay_made", "qe_made", "ke_made", "kdec_made"))
        v_turned, v_made, kd_turned, kd_made = (
            signal(n, 4) for n in ("v_turned", "v_made", "kd_turned", "kd_made"))
        rnn_q, rnn_xi, rnn_a, root_made, rnn_beta, rnn_u = (
            signal(n, 2) for n in ("rnn_q", "rnn_xi", "rnn_a", "root_made", "rnn_beta", "rnn_u"))
        scan_made = signal("scan_made", 8)
        hsum_made, yrnn_made, sgate_made, gelu_made = (
            signal(n, 1) for n in ("hsum_made", "yrnn_made", "sgate_made", "gelu_made"))
        U_GROUPS = [range(0, 4), range(4, NCH - 1)]
        u_mm, state_made = signal("u_mm", NDP * 2), signal("state_made", NDP * (NCH - 1) * 2)
        score_mm, score_kept, o_mm = signal("score_mm", 8), signal("score_kept", 8), signal("o_mm", HEADS)

        def chunk_of(d, j):
            return j if d == 0 else NCH - 1 - j

        block = ctx.enter_context(nc.Block())

        @block.sync
        def _(sp_eng):

            def load_block(l, b, s, src, units=8):
                gap = free_after(b, RAW) if isinstance(b, int) else b + (1 - RAW)
                sp_eng.wait_ge(lo_made.sem, lo_made.after(l, gap))
                sp_eng.dma_start(raw[:, s, 0:units * P].rearrange("p (k c) -> p k c", k=units),
                                 src).then_inc(loaded[s].sem, 16)

            def cols(w, l, c):
                return w[l, :, bass.ds(c, P)].rearrange("(k p) c -> p k c", p=P)

            def first_blocks(l, layer):
                for b in range(RAW):
                    load_block(l, b, slot(b, RAW), cols(w_in, layer, IN_COLS[b]))

            def load_x(n):
                part = slice(n * 2 * P, (n + 1) * 2 * P)
                sp_eng.dma_start(xs[:, :, part], x[0, :, part].rearrange("(t p) d -> p t d", p=P)) \
                    .then_inc(s_x[n], 16)

            first_blocks(0, 0)
            load_x(0)
            for name, src in (("mix_pre", mix_norm_pre), ("mix_post", mix_norm_post),
                              ("ffn_pre", ffn_norm_pre), ("ffn_post", ffn_norm_post),
                              ("conv_b", conv_b), ("rnn_norm", rnn_out_norm), ("gla_norm", gla_out_norm)):
                n = src.shape[1] // P
                sp_eng.dma_start(prow[rows[name]:rows[name] + n, :, :],
                                 src.rearrange("l (t p) -> t l p", p=P)).then_inc(s_par, 16)
            for name, src in (("conv_w", conv_w), ("b_a", lru_b_a), ("b_x", lru_b_x),
                              ("lam", lru_lambda), ("gla_b", gla_b_gate)):
                n = src.shape[1] * src.shape[2] // P
                sp_eng.dma_start(prow[rows[name]:rows[name] + n, :, :],
                                 src.rearrange("l w (t p) -> (w t) l p", p=P)).then_inc(s_par, 16)

            for n in range(1, NC // 2):
                load_x(n)

            with sp_eng.Fori(0, LAYERS) as l:
                for b in range(RAW, LR):
                    load_block(l, b, slot(b, RAW), cols(w_in, l, IN_COLS[b]))
                sp_eng.wait_ge(lru_zeroed.sem, lru_zeroed.after(l, 2))
                for g, w in enumerate((lru_w_a, lru_w_x)):
                    for odd in range(2):
                        src = w[l].rearrange("r (t q) i j -> q i (r t) j", q=2)[odd]
                        dst = lru_w.rearrange("p g r t j -> p g (r t) j")
                        sp_eng.dma_start(dst[64 * odd:64 * odd + 64, g, :, 64 * odd:64 * odd + 64],
                                         src).then_inc(lru_loaded.sem, 16)
                for d in range(2):
                    sp_eng.dma_start(mix[96 + RANK * d:96 + RANK * (d + 1), 33, d * DK_ALL:(d + 1) * DK_ALL],
                                     gla_w_gate[l, d]).then_inc(gla_loaded.sem, 16)
                for b in range(LR, B_OUT):
                    load_block(l, b, slot(b, RAW), cols(w_in, l, IN_COLS[b]))
                for c in range(NC):
                    load_block(l, B_OUT + c, slot(B_OUT + c, RAW), cols(w_out, l, c * P))
                with sp_eng.Fori(0, NF // 2) as i:
                    for j in range(2):
                        load_block(l, i * 4 + (B_FF + 2 * j), 0, cols(w_ffn_gate, l, i * (2 * P) + j * P))
                        load_block(l, i * 4 + (B_FF + 2 * j + 1), 1, cols(w_ffn_up, l, i * (2 * P) + j * P))
                for c in range(NC):
                    k = 0
                    for j, units in enumerate(DOWN_UNITS):
                        b = B_DOWN + 3 * c + j
                        load_block(l, b, slot(b, RAW), w_ffn_down[l, k * P:(k + units) * P, bass.ds(c * P, P)]
                                   .rearrange("(k p) c -> p k c", p=P), units)
                        k += units
                with sp_eng.If(l < LAYERS - 1):
                    first_blocks(l + 1, nc.s_assert_within(
                        l + 1, 1, LAYERS - 1, skip_runtime_bounds_check_because="the last layer is left out"))

            for n in range(2 * NS):
                half, t = divmod(n, NS)
                sp_eng.wait_ge(y_rows, n + 1)
                sp_eng.dma_start(out[0, t * P:(t + 1) * P, half * 512:(half + 1) * 512],
                                 xs[:, t, half * 512:(half + 1) * 512]).then_inc(s_out, 16)
            sp_eng.wait_ge(s_out, 16 * 2 * NS)

        @block.gpsimd
        def _(pool):
            pool.memset(started[:], 0.0).then_inc(lo_made.sem, RAW)
            pool.memset(ones[:], 1.0).then_inc(const_made, 1)
            pool.memset(ident[:], 0.0).then_inc(const_made, 1)
            pool.memset(pre_gain[:, LAYERS, :], 0.0).then_inc(const_made, 1)
            pool.memset(reset[:], 1.0).then_inc(const_made, 1)
            pool.memset(mask32, 1.0).then_inc(const_made, 1)
            pool.wait_ge(const_made, 5)
            pool.affine_select(out=ident[:], in_=ident[:], compare_op=ALU.not_equal, fill=1.0, base=0,
                               pattern=[[-1, P]], channel_multiplier=1).then_inc(const_made, 1)
            pool.memset(reset[:].rearrange("p (n t) -> p n t", t=CHUNK)[:, :, 0:1], 0.0).then_inc(const_made, 1)
            for d in range(2):
                pool.affine_select(out=mask32[:, d, :], in_=mask32[:, d, :], compare_op=ALU.is_ge, fill=0.0, base=0,
                                   pattern=[[1 - 2 * d, P]], channel_multiplier=2 * d - 1).then_inc(const_made, 1)
            pool.wait_ge(const_made, 9)
            for d in range(2):
                pool.memset(mask32[64 * d:64 * d + 64, d, 64 * (1 - d):64 * (1 - d) + 64], 0.0).then_inc(const_made, 1)

            pool.wait_ge(const_made, 11)

            def rest(l, b, b_slot, s, units=8):
                pool.wait_ge(hi_made.sem, hi_made.after(l, b + 1))
                pool.wait_ge(block_used.sem, block_used.after(l, b_slot))
                pool.tensor_tensor(w_lo[:, s, 0:units * P], raw[:, s % RAW, 0:units * P],
                                   w_hi[:, s, 0:units * P].bitcast(F32), ALU.subtract).then_inc(lo_made.sem, 1)

            def rest_of(l, b, units=8):
                rest(l, b, free_after(b, SPL), slot(b, SPL), units)

            def sum_squares(l, n_sq, n_acc):
                for c in range(1, NC):
                    pool.wait_ge(xsq_made.sem, xsq_made.after(l, n_sq + c + 1))
                    if c > 1:
                        pool.wait_ge(xacc_made.sem, xacc_made.after(l, n_acc + c - 1))
                    pool.tensor_tensor(y32[:, 0, :], sq[:, 0, :] if c == 1 else y32[:, 0, :], sq[:, c % 2, :],
                                       ALU.add).then_inc(xacc_made.sem, 1)

            def first_blocks(l):
                for b in range(SPL):
                    rest_of(l, b)

            first_blocks(0)
            sum_squares(0, -NC, 1 - NC)
            with pool.Fori(0, LAYERS) as l:
                for b in range(SPL, B_OUT + NC + SPL):
                    rest_of(l, b)
                sum_squares(l, 0, 0)
                with pool.Fori(1, NF // 2) as i:
                    for j in range(4):
                        b = i * 4 + (B_FF + j)
                        rest(l, b, b + (1 - SPL), j)
                for b in range(B_DOWN, NB):
                    rest_of(l, b, DOWN_UNITS[(b - B_DOWN) % 3])
                with pool.If(l < LAYERS - 1):
                    first_blocks(l + 1)
                    sum_squares(l, NC, NC - 1)

        @block.scalar
        def _(act):
            def head(l, b, s, n_loads, gap, units=8):
                ring = loaded[s % RAW]
                act.wait_ge(ring.sem, ring.after(l, n_loads * 16 + 16))
                act.wait_ge(block_used.sem, block_used.after(l, gap))
                act.activation(w_hi[:, s, 0:units * P], raw[:, s % RAW, 0:units * P],
                               ACT.Copy).then_inc(hi_made.sem, 1)

            def head_of(l, b, units=8):
                head(l, b, slot(b, SPL), loads_before(b), free_after(b, SPL), units)

            def inverse_rms(l, n, mms, features, dst=rstd):
                act.wait_ge(stat_mm.sem, stat_mm.after(l, mms))
                act.activation(dst[:], bank[STAT][:], ACT.Ln, bias=EPS, scale=1.0 / features) \
                    .then_inc(stat_read.sem, 1)
                act.wait_ge(stat_read.sem, stat_read.after(l, n + 1))
                act.activation(dst[:], dst[:], ACT.Exp, scale=-0.5).then_inc(rstd_made.sem, 1)

            def split_and_square_x(l, n_x, n_acc, gain, blocks={}):
                for c in range(NC):
                    if c in blocks:
                        head_of(l, blocks[c])
                    act.wait_ge(x_made.sem, x_made.after(l, n_x + c + 1))
                    act.activation(h_hi[:, c, :], xT[:, c, :], ACT.Copy, scale=gain(c)).then_inc(y_hi.sem, 1)
                    if c >= 2:
                        act.wait_ge(xacc_made.sem, xacc_made.after(l, n_acc + max(1, c - 2)))
                    act.activation(sq[:, c % 2, :], xT[:, c, :], ACT.Square).then_inc(xsq_made.sem, 1)

            def split_hi(l, c, n):
                act.wait_ge(y32_made.sem, y32_made.after(l, n + 1))
                act.activation(h_hi[:, c, :], y32[:, c % 2, :], ACT.Copy).then_inc(y_hi.sem, 1)

            def square_of_output(l, c, n_m, n_acc):
                act.wait_ge(m_made.sem, m_made.after(l, n_m + c + 1))
                if c >= 2:
                    act.wait_ge(acc_made.sem, acc_made.after(l, n_acc + c - 1))
                act.activation(sq[:, c % 2, :], m[:, c, :], ACT.Square).then_inc(sq_made.sem, 1)

            def square_of_last(l, n_acc):
                act.wait_ge(block_used.sem, block_used.after(l, NB if n_acc else B_FF))
                act.wait_ge(acc_made.sem, acc_made.after(l, n_acc + NC - 2))
                act.activation(sq[:, (NC - 1) % 2, :], bank[OUT_BANKS[(NC - 1) % 2]][:], ACT.Square) \
                    .then_inc(sq_made.sem, 1)

            act.preload_act_table_set(EXP_LN)
            act.wait_ge(const_made, 1)
            for n, signalled in enumerate((stat_read, z_abs, z_exp, z_log)):
                act.activation(begun[:, n:n + 1], ones[:, 0:1], ACT.Copy).then_inc(signalled.sem, 1)
            for b in range(RAW):
                head_of(0, b)
            act.wait_ge(gain_made, 1)
            split_and_square_x(0, -NC, 1 - NC, lambda c: pre_gain[:, 0, c:c + 1], {1: 2, 2: 3})

            act.activation(sp[:, 0], pcol[:, :, rows["lam"]:rows["lam"] + 2 * NR], ACT.Abs).then_inc(sp_exp, 1)
            act.wait_ge(sp_exp, 1)
            act.activation(sp[:, 1], sp[:, 0], ACT.Exp, scale=-1.0).then_inc(sp_exp, 1)

            with act.Fori(0, LAYERS) as l:
                inverse_rms(l, 0, 1, D, rstd_h)
                for b in range(SPL, QK + 4 + SPL - 1):
                    head_of(l, b)

                act.wait_ge(par_made.sem, par_made.after(l, 2))
                for c in range(NR):
                    for d in range(2):
                        for g, (dst, col) in enumerate(((rnn_r, "b_a"), (rnn_i, "b_x"))):
                            n = 4 * c + 2 * d + g
                            act.wait_ge(lru_mm.sem, lru_mm.after(l, n + 1))
                            k = rows[col] + d * NR + c
                            act.activation(dst[:, d * NR + c, :], bank[LRU_BANKS[2 * d + g]][:], ACT.Sigmoid,
                                           bias=par[:, k:k + 1]).then_inc(lru_sig.sem, 1)
                act.wait_ge(lru_sig.sem, lru_sig.after(l, 16))
                for n in range(2 * NR):
                    act.activation(rnn_t[:, n, :], rnn_r[:, n, :], ACT.Tanh,
                                   scale=par[:, COL_TANH + n:COL_TANH + n + 1]).then_inc(tanh_made.sem, 1)
                head_of(l, V + 3)

                for k in range(NDP):
                    act.wait_ge(z_min.sem, z_min.after(l, k + 1))
                    act.activation(qe[:, k, :], bank[T_BANKS[k]][:], ACT.Abs,
                                   bias=par[:, rows["gla_b"] + k:rows["gla_b"] + k + 1]).then_inc(z_abs.sem, 1)
                act.preload_act_table_set(EXP_LN)
                act.wait_ge(z_abs.sem, z_abs.after(l, NDP))
                act.activation(qe, qe, ACT.Exp, scale=-1.0).then_inc(z_exp.sem, NDP)
                head_of(l, V + 4)
                act.wait_ge(z_exp.sem, z_exp.after(l, NDP))
                act.activation(qe, qe, ACT.Ln, bias=1.0).then_inc(z_log.sem, NDP)
                act.wait_ge(tanh_made.sem, tanh_made.after(l, 8))
                for n in range(NR):
                    act.activation(rnn_r[:, n, :], rnn_r[:, n, :], ACT.Exp,
                                   scale=par[:, COL_EXP + n:COL_EXP + n + 1]).then_inc(r_exp.sem, 1)
                head_of(l, V + 5)
                for n in range(NR, 2 * NR):
                    act.activation(rnn_r[:, n, :], rnn_r[:, n, :], ACT.Exp,
                                   scale=par[:, COL_EXP + n:COL_EXP + n + 1]).then_inc(r_exp.sem, 1)
                head_of(l, V + 6)
                head_of(l, V + 7)

                for k in range(NDP):
                    act.wait_ge(b_made.sem, b_made.after(l, k + 1))
                    act.activation(qe[:, k, :], kdec[:, k, :], ACT.Exp, scale=1.0 / TAU).then_inc(eb_made.sem, 1)
                    if k == 0:
                        act.wait_ge(v_turned.sem, v_turned.after(l, 4))
                    act.activation(ke[:, k, :], kdec[:, k, :], ACT.Exp, scale=-1.0 / TAU).then_inc(enb_made.sem, 1)
                    if k == 1:
                        head_of(l, G + 4)
                head_of(l, G + 5)
                for d in range(2):
                    act.wait_ge(rnn_q.sem, rnn_q.after(l, d + 1))
                    act.activation(rnn_t[:, d * NR:(d + 1) * NR, :], rnn_t[:, d * NR:(d + 1) * NR, :],
                                   ACT.Sqrt).then_inc(root_made.sem, 1)
                    head_of(l, G + 6 + d)
                act.wait_ge(in_made.sem, in_made.after(l, GR))
                act.activation(sg, sg, ACT.Silu).then_inc(sgate_made.sem, 1)
                act.wait_ge(in_made.sem, in_made.after(l, B_OUT))
                act.activation(gate_r, gate_r, ACT.Gelu_apprx_tanh).then_inc(gelu_made.sem, 1)
                head_of(l, B_OUT)
                head_of(l, B_OUT + 1)

                act.preload_act_table_set(EXP_LN)

                act.wait_ge(yrnn_made.sem, yrnn_made.after(l, 1))
                for c in range(NR):
                    if c >= 2:
                        act.wait_ge(stat_mm.sem, stat_mm.after(l, ST_RNN + c - 1))
                    act.activation(sq[:, c % 2, :], y_rnn[:, c, :], ACT.Square).then_inc(sq_made.sem, 1)
                inverse_rms(l, 1, ST_HEAD, D_RNN)
                head_of(l, B_OUT + 2)
                head_of(l, B_OUT + 3)
                for c in range(NR):
                    split_hi(l, c, H_Y + c)
                for h in range(HEADS):
                    act.wait_ge(o_mm.sem, o_mm.after(l, h + 1))
                    act.activation(sq[:, h % 2, :], bank[O_BANKS[h]][:], ACT.Square).then_inc(sq_made.sem, 1)
                    if h:
                        split_hi(l, NR + h - 1, NR + h - 1)
                    if h:
                        act.wait_ge(head_scaled.sem, head_scaled.after(l, h))
                    else:
                        act.wait_ge(y32_made.sem, y32_made.after(l, NR))
                    inverse_rms(l, 2 + h, ST_HEAD + h + 1, DV)
                split_hi(l, NC - 1, NC - 1)

                for c in range(NC):
                    head_of(l, B_OUT + c + SPL)
                    square_of_output(l, c, 0, 0) if c < NC - 1 else square_of_last(l, 0)
                inverse_rms(l, 6, ST_POST + 2, D)

                split_and_square_x(l, 0, 0, lambda c: par[:, rows["ffn_pre"] + c:rows["ffn_pre"] + c + 1])
                inverse_rms(l, 7, ST_PRE1 + 1, D, rstd_h)

                act.preload_act_table_set(SILU)
                with act.Fori(0, NF // 2) as i:
                    for j in range(2):
                        f = i * 2 + j
                        b = i * 4 + (B_FF + SPL + 2 * j)
                        loads = [i * 2 + loads_before(B_FF + SPL + 2 * j + n) for n in range(2)]
                        head(l, b, 2 * j, loads[0], b + (1 - SPL))
                        act.wait_ge(gate_scaled.sem, gate_scaled.after(l, f + 1))
                        act.activation(sq[:, j, :], sq[:, j, :], ACT.Silu).then_inc(silu_made.sem, 1)
                        head(l, b + 1, 2 * j + 1, loads[1], b + (2 - SPL))
                        act.wait_ge(g32_made.sem, g32_made.after(l, f + 1))
                        act.activation(g_hi[:, bass.ds(f, 1), :], y32[:, j:j + 1, :], ACT.Copy) \
                            .then_inc(ghi_made.sem, 1)
                for b in range(B_DOWN + SPL, NB):
                    head_of(l, b, DOWN_UNITS[(b - B_DOWN) % 3])
                    c, n = divmod(b - SPL - B_DOWN, 3)
                    if n == 2:
                        square_of_output(l, c, NC, NC - 1)
                act.preload_act_table_set(EXP_LN)
                with act.If(l < LAYERS - 1):
                    head_of(l + 1, 0)
                square_of_output(l, NC - 2, NC, NC - 1)
                with act.If(l < LAYERS - 1):
                    head_of(l + 1, 1)
                    head_of(l + 1, 2)
                square_of_last(l, NC - 1)
                with act.If(l < LAYERS - 1):
                    head_of(l + 1, 3)
                inverse_rms(l, 8, N_ST, D)
                with act.If(l < LAYERS - 1):
                    split_and_square_x(l, NC, NC - 1, lambda c: next_gain[:, c:c + 1])

        @block.tensor
        def _(pe):
            def passes(psum, s, unit, a_hi, a_lo, first, last):
                hi, lo = (w[:, s, unit * P:(unit + 1) * P] for w in (w_hi, w_lo))
                pe.matmul(psum, hi, a_hi, start=first, stop=False)
                pe.matmul(psum, hi, a_lo, start=False, stop=False)
                return pe.matmul(psum, lo, a_hi, start=False, stop=last)

            def project(l, b, s, psum, n_h=None):
                pe.wait_ge(lo_made.sem, lo_made.after(l, b + 1))
                if n_h is not None:
                    pe.wait_ge(y_lo.sem, y_lo.after(l, n_h))
                for k in range(NC):
                    last = passes(bank[psum][:], s, k, h_hi[:, k, :], h_lo[:, k, :], k == 0, k == NC - 1)
                last.then_inc(block_used.sem, 1)

            def project_first(l, b, n_h, n_acc, n_read):
                early = NC - 2
                pe.wait_ge(lo_made.sem, lo_made.after(l, b + SPL))
                for k in range(early):
                    pe.wait_ge(y_lo.sem, y_lo.after(l, n_h + k + 1))
                    for n in range(SPL):
                        passes(bank[FIRST[n]][:], n, k, h_hi[:, k, :], h_lo[:, k, :], k == 0, False)
                pe.wait_ge(y_lo.sem, y_lo.after(l, n_h + NC))
                for n in range(SPL):
                    for k in range(early, NC):
                        last = passes(bank[FIRST[n]][:], n, k, h_hi[:, k, :], h_lo[:, k, :], False, k == NC - 1)
                    last.then_inc(block_used.sem, 1)
                    if n == 1:
                        stat(l, n_read, y32[:, 0, :], xacc_made.sem, xacc_made.after(l, n_acc), True, True)

            def stat(l, n_read, src, wait_sem, wait_value, first, last):
                if first:
                    pe.wait_ge(stat_read.sem, stat_read.after(l, n_read))
                pe.wait_ge(wait_sem, wait_value)
                pe.matmul(bank[STAT][:], ones[:], src, start=first, stop=last).then_inc(stat_mm.sem, 1)

            def turn4(dst, srcs, size=P):
                for i, src in enumerate(srcs):
                    last = pe.transpose(dst[:, i * P:(i + 1) * P], src, ident[:])
                return last

            pe.wait_ge(const_made, 1)
            pe.matmul(bank[6][:, 0:P], ones[:], ones[:], start=True, stop=True).then_inc(block_used.sem, SPL)
            pe.matmul(bank[6][:, 0:P], ones[:], ones[:], start=True, stop=True).then_inc(z_mm.sem, z_mm.before)
            pe.wait_ge(const_made, 6)
            pe.wait_ge(s_par, 16 * 12)
            for l in range(LAYERS):
                pe.transpose(bank[2 + l][:, 0:n_rows], prow[:, l, :], ident[0:n_rows, 0:n_rows]).then_inc(par_turned, 1)
            for c in range(NC):
                pe.wait_ge(s_x[c // 2], 16)
                if c >= 2:
                    pe.wait_ge(x_made.sem, c - 1)
                for t in range(NS):
                    last = pe.transpose(bank[X_BANKS[c % 2]][:, t * P:(t + 1) * P], xs[:, t, c * P:(c + 1) * P], ident[:])
                last.then_inc(x_turned, 1)

            with pe.Fori(0, LAYERS) as l:
                def project_in(b):
                    if b < V:
                        pe.wait_ge(in_made.sem, in_made.after(l, b % 2 + 1 if b < QK + 1 else b - 1))
                    else:
                        pe.wait_ge(in_made.sem, in_made.after(l, b - 1))
                    project(l, b, slot(b, SPL), PROJ[b % 2])

                project_first(l, XR, -NC, 0, 0)
                for b in range(LR, V):
                    project_in(b)

                pe.wait_ge(lru_loaded.sem, lru_loaded.after(l, 64))
                for c in range(NR):
                    pe.wait_ge(conv_step.sem, conv_step.after(l, 4 * (c + 1)))
                    for d in range(2):
                        for g in range(2):
                            if c:
                                pe.wait_ge(lru_sig.sem, lru_sig.after(l, 4 * (c - 1) + 2 * d + g + 1))
                            pe.matmul(bank[LRU_BANKS[2 * d + g]][:], lru_w[:, g, d, c, :], xc[:, c, :],
                                      start=True, stop=True).then_inc(lru_mm.sem, 1)
                pe.wait_ge(gla_loaded.sem, gla_loaded.after(l, 32))
                for k in range(NDP):
                    d, pair = divmod(k, PAIRS)
                    if k:
                        pe.wait_ge(lru_sig.sem, lru_sig.after(l, 12 + k))
                    pe.matmul(bank[T_BANKS[k]][:], gla_w[:, d * DK_ALL + pair * P:d * DK_ALL + (pair + 1) * P], lr,
                              start=True, stop=True).then_inc(z_mm.sem, 1)

                for b in range(V, G):
                    project_in(b)
                pe.wait_ge(in_made.sem, in_made.after(l, G))
                pe.wait_ge(z_abs.sem, z_abs.after(l, NDP))
                for t in range(NS):
                    turn4(bank[T_BANKS[t]], [vT[:, c, t * P:(t + 1) * P] for c in range(HEADS)]) \
                        .then_inc(v_turned.sem, 1)
                for b in range(G, GR):
                    project_in(b)
                pe.wait_ge(v_made.sem, v_made.after(l, 4))
                for k in range(NDP):
                    pe.wait_ge(kdec_made.sem, kdec_made.after(l, k + 1))
                    turn4(bank[T_BANKS[k]], [kdec[:, k, t * P:(t + 1) * P] for t in range(NS)]) \
                        .then_inc(kd_turned.sem, 1)
                for b in range(GR, B_OUT):
                    project_in(b)

                pe.wait_ge(kd_made.sem, kd_made.after(l, 4))
                for k in range(NDP):
                    d, pair = divmod(k, PAIRS)
                    for g, js in enumerate(U_GROUPS):
                        if k:
                            pe.wait_ge(state_made.sem, state_made.after(l, 2 * ((k - 1) * (NCH - 1) + js[-1] + 1)))
                        for j in js:
                            t, half = divmod(chunk_of(d, j), 2)
                            p0, c0 = CHUNK * half, (j - js[0]) // 2 * 2 * DV
                            last = pe.matmul(bank[U_BANKS[g][j % 2]][:, c0:c0 + 2 * DV], kdT[p0:p0 + CHUNK, k, t, :],
                                             v[p0:p0 + CHUNK, t, 2 * pair * DV:2 * (pair + 1) * DV],
                                             start=True, stop=True)
                        last.then_inc(u_mm.sem, 1)

                def score(h):
                    pair, odd = divmod(h, 2)
                    if h >= 2:
                        pe.wait_ge(score_kept.sem, score_kept.after(l, 2 * (h - 1)))
                    for d in range(2):
                        for t in range(NS):
                            a, b = (z[DK * odd:DK * odd + DK, d * PAIRS + pair, t * P:(t + 1) * P] for z in (ke, qe))
                            last = pe.matmul(bank[S_BANKS[odd][d]][:, t * P:(t + 1) * P], a, b, start=True, stop=True)
                        last.then_inc(score_mm.sem, 1)

                def output(h):
                    pair, odd = divmod(h, 2)
                    dst = bank[O_BANKS[h]]
                    pe.wait_ge(score_kept.sem, score_kept.after(l, 2 * h + 2))
                    for d in range(2):
                        for t in range(NS):
                            pe.matmul(dst[:, t * P:(t + 1) * P], v[:, t, h * DV:(h + 1) * DV],
                                      scores[:, 2 * d + h % 2, t * P:(t + 1) * P],
                                      start=(d == 0 and t == 0), stop=False, skip_group_check=True)
                    for d in range(2):
                        for j in range(NCH - 1):
                            i0 = chunk_of(d, j + 1) * CHUNK
                            last = pe.matmul(dst[:, i0:i0 + CHUNK],
                                             states[DK * odd:DK * odd + DK, d * PAIRS + pair, j, :],
                                             qe[DK * odd:DK * odd + DK, d * PAIRS + pair, i0:i0 + CHUNK],
                                             start=False, stop=(d == 1 and j == NCH - 2), skip_group_check=True)
                    last.then_inc(o_mm.sem, 1)

                def head_stat(h):
                    stat(l, 2 + h, sq[:, h % 2, :], sq_made.sem, sq_made.after(l, SQ_HEAD + h + 1), True, True)

                def project_out(b, ks):
                    for k in ks:
                        pe.wait_ge(y_lo.sem, y_lo.after(l, H_Y + k + 1))
                        last = passes(bank[OUT_BANKS[(b - B_OUT) % 2]][:], slot(b, SPL), k, h_hi[:, k, :], h_lo[:, k, :],
                                      k == 0, k == NC - 1)
                    if k == NC - 1:
                        last.then_inc(block_used.sem, 1)

                pe.wait_ge(in_made.sem, in_made.after(l, B_OUT))
                score(0)
                for c in range(NR):
                    stat(l, 1, sq[:, c % 2, :], sq_made.sem, sq_made.after(l, SQ_RNN + c + 1), c == 0, c == NR - 1)
                pe.wait_ge(state_made.sem, state_made.after(l, state_made.per_layer))
                score(1)
                output(0)
                score(2)
                head_stat(0)
                output(1)
                score(3)
                head_stat(1)
                output(2)
                head_stat(2)
                output(3)
                pe.wait_ge(lo_made.sem, lo_made.after(l, B_OUT + 2))
                project_out(B_OUT, range(NR))
                head_stat(3)
                project_out(B_OUT + 1, range(NR))
                project_out(B_OUT, range(NR, NC))
                project_out(B_OUT + 1, range(NR, NC))
                for b in range(B_OUT + 2, B_FF):
                    pe.wait_ge(m_made.sem, m_made.after(l, b - B_OUT - 1))
                    pe.wait_ge(lo_made.sem, lo_made.after(l, b + 1))
                    project_out(b, range(NC))
                stat(l, 6, y32[:, 0, :], acc_made.sem, acc_made.after(l, NC - 1), True, False)
                stat(l, 6, sq[:, (NC - 1) % 2, :], sq_made.sem, sq_made.after(l, SQ_POST + NC), False, True)

                project_first(l, B_FF, H_X1, NC - 1, 7)
                with pe.Fori(1, NF // 2) as i:
                    for j in range(2):
                        pe.wait_ge(gate_scaled.sem, gate_scaled.after(l, i * 2 + (j - 1)))
                        project(l, i * 4 + (B_FF + 2 * j), 2 * j, 2 * j)
                        pe.wait_ge(up_scaled.sem, up_scaled.after(l, i * 2 + (j - 1)))
                        project(l, i * 4 + (B_FF + 2 * j + 1), 2 * j + 1, 2 * j + 1)
                with pe.Fori(0, NC // 4) as i:
                    for j in range(4):
                        psum = OUT_BANKS[j % 2]
                        pe.wait_ge(m_made.sem, m_made.after(l, i * 4 + (NC + j - 1)))
                        k = 0
                        for n, units in enumerate(DOWN_UNITS):
                            pe.wait_ge(lo_made.sem, lo_made.after(l, i * 12 + (B_DOWN + 3 * j + n + 1)))
                            pe.wait_ge(glo_made.sem, glo_made.after(l, k + units - (n == 2)))
                            for u in range(units):
                                if k == NF - 1:
                                    pe.wait_ge(glo_made.sem, glo_made.after(l, NF))
                                last = passes(bank[psum][:], (3 * j + n) % SPL, u, g_hi[:, k, :], g_lo[:, k, :],
                                              k == 0, k == NF - 1)
                                k += 1
                            last.then_inc(block_used.sem, 1)
                stat(l, 8, y32[:, 0, :], acc_made.sem, acc_made.after(l, 2 * (NC - 1)), True, False)
                stat(l, 8, sq[:, (NC - 1) % 2, :], sq_made.sem, sq_made.after(l, SQ_POST1 + NC), False, True)

            for n in range(2 * NS):
                half, t = divmod(n, NS)
                if t == 0:
                    pe.wait_ge(x_made.sem, x_made.after(LAYERS, 4 * half + 4 - NC))
                if n >= 4:
                    pe.wait_ge(y_rows, n - 3)
                turn4(bank[n % 4], [xT[:, 4 * half + i, t * P:(t + 1) * P] for i in range(4)]) \
                    .then_inc(y_turned, 1)

        @block.vector
        def _(dve):
            def rest_of_x(l, c, n, gain):
                dve.wait_ge(y_hi.sem, y_hi.after(l, n + c + 1))
                dve.scalar_tensor_tensor(h_lo[:, c, :], xT[:, c, :], gain, h_hi[:, c, :].bitcast(F32),
                                         ALU.mult, ALU.subtract).then_inc(y_lo.sem, 1)

            dve.memset(carrier[:, 0:1], 0.0).then_inc(m_made.sem, 2)
            dve.memset(carrier[:, 2:3], 0.0).then_inc(z_min.sem, 1)
            dve.wait_ge(const_made, 11)
            dve.tensor_copy(mask[:], mask32).then_inc(masks_made, 1)
            for l in range(LAYERS):
                dve.wait_ge(par_turned, l + 1)
                dve.tensor_copy(pcol[:, l, 0:n_rows], bank[2 + l][:, 0:n_rows]).then_inc(pcol_made, 1)
            dve.wait_ge(pcol_made, LAYERS)
            dve.tensor_copy(pre_gain[:, 0:LAYERS, :],
                            pcol[:, :, rows["mix_pre"]:rows["mix_pre"] + NC]).then_inc(gain_made, 1)
            dve.wait_ge(gain_made, 1)
            for c in range(NC + 1):
                if c < NC:
                    dve.wait_ge(x_turned, c + 1)
                    dve.tensor_copy(xT[:, c, :], bank[X_BANKS[c % 2]][:]).then_inc(x_made.sem, 1)
                if c:
                    rest_of_x(0, c - 1, -NC, pre_gain[:, 0, c - 1:c])

            done = [0]

            def step(ins):
                done[0] += 1
                ins.then_inc(sp_step, 1)
                dve.wait_ge(sp_step, done[0])

            lam = pcol[:, :, rows["lam"]:rows["lam"] + 2 * NR]
            dve.wait_ge(sp_exp, 2)
            step(dve.tensor_scalar(sp[:, 2], sp[:, 1], 2.0, None, ALU.add))
            step(dve.reciprocal(sp[:, 3], sp[:, 2]))
            step(dve.tensor_tensor(sp[:, 4], sp[:, 1], sp[:, 3], ALU.mult))
            step(dve.tensor_tensor(sp[:, 5], sp[:, 4], sp[:, 4], ALU.mult))
            step(dve.tensor_scalar(sp[:, 6], sp[:, 5], 1.0 / 19, None, ALU.mult))
            for odd in range(17, 1, -2):
                step(dve.scalar_tensor_tensor(sp[:, 6], sp[:, 6], 1.0 / odd, sp[:, 5], ALU.add, ALU.mult))
            step(dve.scalar_tensor_tensor(sp[:, 6], sp[:, 6], 1.0, sp[:, 4], ALU.add, ALU.mult))
            step(dve.tensor_scalar(sp[:, 7], lam, -1.0, 0.0, ALU.mult, ALU.max))
            step(dve.scalar_tensor_tensor(sp[:, 7], sp[:, 6], 2.0, sp[:, 7], ALU.mult, ALU.add))
            dve.tensor_scalar(pcol[:, :, COL_TANH:COL_TANH + 2 * NR], sp[:, 7], LRU_C / 2, None,
                              ALU.mult).then_inc(pcol_made, 1)
            dve.tensor_scalar(pcol[:, :, COL_EXP:COL_EXP + 2 * NR], sp[:, 7], -LRU_C, None,
                              ALU.mult).then_inc(pcol_made, 1)
            dve.wait_ge(pcol_made, LAYERS + 2)

            def col(name, k=0):
                k += rows[name]
                return par[:, k:k + 1]

            def split_lo(l, c, n):
                dve.wait_ge(y_hi.sem, y_hi.after(l, n + 1))
                dve.tensor_tensor(h_lo[:, c, :], y32[:, c % 2, :], h_hi[:, c, :].bitcast(F32),
                                  ALU.subtract).then_inc(y_lo.sem, 1)

            def normalise(l, n, chunks, src, gain, n_rstd):
                dve.wait_ge(rstd_made.sem, rstd_made.after(l, n_rstd + 1))
                for c in range(chunks):
                    if c >= 2:
                        dve.wait_ge(y_lo.sem, y_lo.after(l, n + c - 1))
                    dve.scalar_tensor_tensor(y32[:, c % 2, :], src[:, c, :], col(gain, c), rstd[:],
                                             ALU.mult, ALU.mult).then_inc(y32_made.sem, 1)
                    if c:
                        split_lo(l, c - 1, n + c - 1)
                split_lo(l, chunks - 1, n + chunks - 1)

            def take_output(l, c, b, psum, n, n_sq):
                dve.wait_ge(block_used.sem, block_used.after(l, b + 1))
                if c == NC - 1:
                    dve.wait_ge(sq_made.sem, sq_made.after(l, n_sq + NC))
                dve.tensor_copy(m[:, c, :], bank[psum][:]).then_inc(m_made.sem, 1)
                if c == NC - 1:
                    return
                dve.wait_ge(sq_made.sem, sq_made.after(l, n_sq + c + 1))
                if c == 0:
                    dve.tensor_copy(y32[:, 0, :], sq[:, 0, :]).then_inc(acc_made.sem, 1)
                else:
                    dve.wait_ge(acc_made.sem, acc_made.after(l, n + c))
                    dve.tensor_tensor(y32[:, 0, :], y32[:, 0, :], sq[:, c % 2, :], ALU.add).then_inc(acc_made.sem, 1)

            def add_branch(l, n, gain, n_rstd, n_h=0, h_gain=None):
                dve.wait_ge(rstd_made.sem, rstd_made.after(l, n_rstd + 1))
                dve.wait_ge(m_made.sem, m_made.after(l, n + NC))
                for c in range(NC + 2):
                    if c < NC:
                        dve.scalar_tensor_tensor(m[:, c, :], m[:, c, :], col(gain, c), rstd[:],
                                                 ALU.mult, ALU.mult).then_inc(m_scaled.sem, 1)
                    if 1 <= c <= NC:
                        dve.wait_ge(m_scaled.sem, m_scaled.after(l, n + c))
                        dve.tensor_tensor(xT[:, c - 1, :], xT[:, c - 1, :], m[:, c - 1, :],
                                          ALU.add).then_inc(x_made.sem, 1)
                    if c >= 2 and h_gain is not None:
                        rest_of_x(l, c - 2, n_h, h_gain(c - 2))

            with dve.Fori(0, LAYERS) as l:
                dve.wait_ge(y_lo.sem, y_lo.after(l, 0))
                dve.tensor_copy(par[:].rearrange("p (o n) -> p o n", o=1), pcol[:, bass.ds(l, 1), :]) \
                    .then_inc(par_made.sem, 1)
                dve.tensor_copy(next_gain[:].rearrange("p (o n) -> p o n", o=1), pre_gain[:, bass.ds(l + 1, 1), :]) \
                    .then_inc(par_made.sem, 1)
                dve.memset(mix[96:P, 33, :], 0.0).then_inc(lru_zeroed.sem, 1)
                dve.memset(at(44, 4), 0.0).then_inc(lru_zeroed.sem, 1)

                def take_in(b, dst, psum=None):
                    rows_ = slice(96, P) if b == LR else slice(0, P)
                    dve.wait_ge(block_used.sem, block_used.after(l, b + 1))
                    dve.tensor_tensor(dst, bank[PROJ[b % 2] if psum is None else psum][rows_, :], rstd_h[rows_, :],
                                      ALU.mult).then_inc(in_made.sem, 1)

                dve.wait_ge(rstd_made.sem, rstd_made.after(l, 1))
                for c in range(NR):
                    take_in(XR + c, x_r[:, c, :], FIRST[c])
                take_in(LR, lr)

                dve.wait_ge(par_made.sem, par_made.after(l, 2))
                for c in range(NR):
                    dve.wait_ge(in_made.sem, in_made.after(l, XR + c + 1))
                    dve.tensor_scalar(xc[:, c, :], x_r[:, c, :], col("conv_w", 2 * NR + c), col("conv_b", c),
                                      ALU.mult, ALU.add).then_inc(conv_step.sem, 1)
                    for n, (tap, shift) in enumerate(((0, -2), (1, -1), (3, 1))):
                        lo, hi = max(0, -shift), SEQ - max(0, shift)
                        dve.wait_ge(conv_step.sem, conv_step.after(l, 4 * c + n + 1))
                        dve.scalar_tensor_tensor(xc[:, c, lo:hi], x_r[:, c, lo + shift:hi + shift],
                                                 col("conv_w", tap * NR + c), xc[:, c, lo:hi],
                                                 ALU.mult, ALU.add).then_inc(conv_step.sem, 1)
                    take_in(QK + c, qk[:, c, :])

                for k in range(NDP):
                    dve.wait_ge(z_mm.sem, z_mm.after(l, k + 1))
                    dve.tensor_scalar(kdec[:, k, :], bank[T_BANKS[k]][:], col("gla_b", k), 0.0,
                                      ALU.add, ALU.min).then_inc(z_min.sem, 1)
                take_in(V, vT[:, 0, :])
                dve.wait_ge(z_log.sem, z_log.after(l, NDP))
                dve.wait_ge(z_min.sem, z_min.after(l, NDP))
                for k in range(NDP):
                    dve.tensor_tensor(kdec[:, k, :], kdec[:, k, :], qe[:, k, :], ALU.subtract) \
                        .then_inc(la_made.sem, 1)
                for k in range(NDP):
                    dve.wait_ge(la_made.sem, la_made.after(l, k + 1))
                    seq = kdec[:, k, :] if k < PAIRS else kdec[:, k, ::-1]
                    dve.tensor_tensor_scan(seq, reset[:], seq, 0.0, ALU.mult, ALU.add).then_inc(b_made.sem, 1)
                    if k == 0:
                        take_in(V + 1, vT[:, 1, :])
                take_in(V + 2, vT[:, 2, :])

                def group(z, d):
                    return z[:, d * NR:(d + 1) * NR, :]

                for d in range(2):
                    dve.wait_ge(r_exp.sem, r_exp.after(l, NR * (d + 1)))
                    r, i, t = group(rnn_r, d), group(rnn_i, d), group(rnn_t, d)
                    dve.scalar_tensor_tensor(r, r, 1.0, t, ALU.add, ALU.mult).then_inc(rnn_q.sem, 1)
                    dve.tensor_tensor(i, i, xc, ALU.mult).then_inc(rnn_xi.sem, 1)
                    dve.wait_ge(rnn_q.sem, rnn_q.after(l, d + 1))
                    dve.tensor_scalar(r, r, -1.0, 1.0, ALU.mult, ALU.add).then_inc(rnn_a.sem, 1)
                    take_in(V + 3, vT[:, 3, :]) if d == 0 else take_in(G, sg[:, 0, :])

                for t in range(NS):
                    dve.wait_ge(v_turned.sem, v_turned.after(l, t + 1))
                    dve.tensor_copy(v[:, t, :], bank[T_BANKS[t]][:]).then_inc(v_made.sem, 1)

                for k in range(NDP):
                    d, pair = divmod(k, PAIRS)
                    dve.wait_ge(eb_made.sem, eb_made.after(l, k + 1))
                    dve.wait_ge(enb_made.sem, enb_made.after(l, k + 1))
                    last = 0 if d else CHUNK - 1
                    dve.tensor_copy(decay[:, k, :], qe[:, k, :].rearrange("p (n t) -> p n t", t=CHUNK)[:, :, last]) \
                        .then_inc(decay_made.sem, 1)
                    dve.tensor_tensor(ke[:, k, :], qk[:, PAIRS + pair, :], ke[:, k, :], ALU.mult).then_inc(ke_made.sem, 1)
                    dve.wait_ge(decay_made.sem, decay_made.after(l, k + 1))
                    dve.scalar_tensor_tensor(qe[:, k, :], qk[:, pair, :], DK ** -0.5, qe[:, k, :],
                                             ALU.mult, ALU.mult).then_inc(qe_made.sem, 1)
                    dve.wait_ge(ke_made.sem, ke_made.after(l, k + 1))
                    chunks = [z[:, k, :].rearrange("p (n t) -> p n t", t=CHUNK) for z in (kdec, ke)]
                    dve.tensor_tensor(chunks[0], chunks[1],
                                      decay[:, k, :].rearrange("p (n o) -> p n o", o=1).to_broadcast([P, NCH, CHUNK]),
                                      ALU.mult).then_inc(kdec_made.sem, 1)
                    if k < 3:
                        take_in(G + 1 + k, sg[:, 1 + k, :])

                for d in range(2):
                    r, i, t = group(rnn_r, d), group(rnn_i, d), group(rnn_t, d)
                    dve.wait_ge(root_made.sem, root_made.after(l, d + 1))
                    dve.wait_ge(rnn_a.sem, rnn_a.after(l, d + 1))
                    dve.scalar_tensor_tensor(t, r, 1.0, t, ALU.add, ALU.mult).then_inc(rnn_beta.sem, 1)
                    dve.wait_ge(rnn_beta.sem, rnn_beta.after(l, d + 1))
                    dve.tensor_tensor(i, i, t, ALU.mult).then_inc(rnn_u.sem, 1)
                    take_in(GR + 2 * d, gate_r[:, 2 * d, :])
                    dve.wait_ge(rnn_u.sem, rnn_u.after(l, d + 1))
                    for c in range(NR):
                        a, u = (z[:, d * NR + c, :] if d == 0 else z[:, d * NR + c, ::-1] for z in (rnn_r, rnn_i))
                        dve.tensor_tensor_scan(u, a, u, 0.0, ALU.mult, ALU.add).then_inc(scan_made.sem, 1)
                    if d == 0:
                        take_in(GR + 1, gate_r[:, 1, :])
                dve.wait_ge(scan_made.sem, scan_made.after(l, 8))
                dve.tensor_tensor(group(rnn_i, 0), group(rnn_i, 0), group(rnn_i, 1), ALU.add).then_inc(hsum_made.sem, 1)
                for k in range(NDP):
                    dve.wait_ge(kd_turned.sem, kd_turned.after(l, k + 1))
                    dve.tensor_copy(kdT[:, k], bank[T_BANKS[k]][:].rearrange("p (t d) -> p t d", t=NS)) \
                        .then_inc(kd_made.sem, 1)
                take_in(GR + 3, gate_r[:, 3, :])
                dve.memset(scores, 0.0).then_inc(scores_zeroed.sem, 1)
                dve.wait_ge(scores_zeroed.sem, scores_zeroed.after(l, 1))
                dve.wait_ge(gelu_made.sem, gelu_made.after(l, 1))
                dve.wait_ge(hsum_made.sem, hsum_made.after(l, 1))
                dve.tensor_tensor(y_rnn, group(rnn_i, 0), gate_r, ALU.mult).then_inc(yrnn_made.sem, 1)

                for k in range(NDP):
                    d = k // PAIRS
                    for j in range(NCH - 1):
                        g, n = j // 4, (k * (NCH - 1) + j) * 2
                        dve.wait_ge(u_mm.sem, u_mm.after(l, 2 * k + g + 1))
                        if j:
                            dve.wait_ge(state_made.sem, state_made.after(l, n))
                        for odd in range(2):
                            p = slice(DK * odd, DK * odd + DK)
                            c0 = (2 * (j % 4 // 2) + odd) * DV
                            u = bank[U_BANKS[g][j % 2]][p, c0:c0 + DV]
                            c = chunk_of(d, j)
                            if j == 0:
                                last = dve.tensor_copy(states[p, k, j, :], u)
                            else:
                                last = dve.scalar_tensor_tensor(states[p, k, j, :], states[p, k, j - 1, :],
                                                                decay[p, k, c:c + 1], u, ALU.mult, ALU.add)
                            last.then_inc(state_made.sem, 1)


                def keep(h):
                    if h >= 2:
                        dve.wait_ge(o_mm.sem, o_mm.after(l, h - 1))
                    for d in range(2):
                        dve.wait_ge(score_mm.sem, score_mm.after(l, 2 * h + d + 1))
                        dve.tensor_copy(carrier[:, 2 * h + d:2 * h + d + 1], ones[:, 0:1])
                        dve.copy_predicated(scores[:, 2 * d + h % 2, :].rearrange("p (t i) -> p t i", t=NS),
                                            mask[:, d:d + 1, :].to_broadcast([P, NS, P]), bank[S_BANKS[h % 2][d]][:].rearrange("p (t i) -> p t i", t=NS)) \
                            .then_inc(score_kept.sem, 1)

                keep(0)
                keep(1)
                dve.wait_ge(block_used.sem, block_used.after(l, B_OUT))
                normalise(l, H_Y, NR, y_rnn, "rnn_norm", 1)
                keep(2)
                dve.wait_ge(sgate_made.sem, sgate_made.after(l, 1))
                for h in range(HEADS):
                    n = H_Y + NR + h
                    dve.wait_ge(rstd_made.sem, rstd_made.after(l, 3 + h))
                    dve.wait_ge(y_lo.sem, y_lo.after(l, n - 1))
                    dve.scalar_tensor_tensor(y32[:, h % 2, :], bank[O_BANKS[h]][:], col("gla_norm"), rstd[:],
                                             ALU.mult, ALU.mult).then_inc(head_scaled.sem, 1)
                    dve.wait_ge(head_scaled.sem, head_scaled.after(l, h + 1))
                    dve.tensor_tensor(y32[:, h % 2, :], y32[:, h % 2, :], sg[:, h, :], ALU.mult) \
                        .then_inc(y32_made.sem, 1)
                    if h == 0:
                        keep(3)
                    split_lo(l, NR + h, n)

                for c in range(NC):
                    take_output(l, c, B_OUT + c, OUT_BANKS[c % 2], 0, SQ_POST)
                add_branch(l, 0, "mix_post", 6, H_X1, lambda c: col("ffn_pre", c))

                with dve.Fori(0, NF // 2) as i:
                    dve.wait_ge(rstd_made.sem, rstd_made.after(l, 8))
                    for j in range(2):
                        f = i * 2 + j
                        b = i * 4 + (B_FF + 2 * j)
                        dve.wait_ge(block_used.sem, block_used.after(l, b + 1))
                        dve.tensor_tensor(sq[:, j, :], bank[2 * j][:], rstd_h[:], ALU.mult) \
                            .then_inc(gate_scaled.sem, 1)
                        dve.wait_ge(block_used.sem, block_used.after(l, b + 2))
                        dve.tensor_tensor(y32[:, j, :], bank[2 * j + 1][:], rstd_h[:], ALU.mult) \
                            .then_inc(up_scaled.sem, 1)
                        dve.wait_ge(silu_made.sem, silu_made.after(l, f + 1))
                        dve.wait_ge(up_scaled.sem, up_scaled.after(l, f + 1))
                        dve.tensor_tensor(y32[:, j, :], sq[:, j, :], y32[:, j, :], ALU.mult) \
                            .then_inc(g32_made.sem, 1)
                        dve.wait_ge(ghi_made.sem, ghi_made.after(l, f + 1))
                        dve.tensor_tensor(g_lo[:, bass.ds(f, 1), :], y32[:, j:j + 1, :],
                                          g_hi[:, bass.ds(f, 1), :].bitcast(F32), ALU.subtract) \
                            .then_inc(glo_made.sem, 1)
                dve.wait_ge(glo_made.sem, glo_made.after(l, NF))
                for c in range(NC):
                    take_output(l, c, B_DOWN + 3 * c + 2, OUT_BANKS[c % 2], NC - 1, SQ_POST1)
                with dve.If(l < LAYERS - 1):
                    add_branch(l, NC, "ffn_post", 8, H_X2, lambda c: next_gain[:, c:c + 1])
                with dve.If(l == LAYERS - 1):
                    add_branch(l, NC, "ffn_post", 8)

            for n in range(2 * NS):
                half, t = divmod(n, NS)
                dve.wait_ge(y_turned, n + 1)
                dve.tensor_copy(xs[:, t, half * 512:(half + 1) * 512], bank[n % 4][:]).then_inc(y_rows, 1)


_INS = ['x', 'mix_norm_pre', 'mix_norm_post', 'w_in', 'conv_w', 'conv_b', 'lru_w_a', 'lru_b_a', 'lru_w_x',
        'lru_b_x', 'lru_lambda', 'rnn_out_norm', 'gla_w_gate', 'gla_b_gate', 'gla_out_norm', 'w_out',
        'ffn_norm_pre', 'ffn_norm_post', 'w_ffn_gate', 'w_ffn_up', 'w_ffn_down']


def kernel(**inputs):
    import numpy as np
    import concourse.bacc as bacc
    from concourse.bass_utils import run_bass_kernel_spmd

    nc = bacc.Bacc("TRN2", target_bir_lowering=False, num_devices=1)
    arrays, args = {}, []
    for name in _INS:
        a = np.ascontiguousarray(inputs[name])
        arrays[f"in_{name}"] = a
        args.append(nc.dram_tensor(f"in_{name}", a.shape, mybir.dt.from_np(a.dtype), kind="ExternalInput").ap())
    shape = arrays["in_x"].shape
    args.append(nc.dram_tensor("out_x", shape, F32, kind="ExternalOutput").ap())
    trunk(nc, *args)
    r = run_bass_kernel_spmd(nc, [arrays], core_ids=[0])
    return r.results[0]["out_x"]
```

```python
from contextlib import ExitStack

import concourse.bass as bass
from concourse import mybir

ALU = mybir.AluOpType
ACT = mybir.ActivationFunctionType
F32 = mybir.dt.float32
F32R = mybir.dt.float32r
U8 = mybir.dt.uint8
BF16 = mybir.dt.bfloat16

P = 128
EPS = 1e-6
LRU_C = 8.0
TAU = 16.0
CHUNK = 64

EXP_LN = "natural_log_exp_and_others"
SILU = "silu_and_others"


class Signal:

    def __init__(self, sem, per_layer, before=0):
        self.sem, self.per_layer, self.before = sem, per_layer, before

    def after(self, layer, n):
        return layer * self.per_layer + (n + self.before)


def trunk(nc, x, mix_norm_pre, mix_norm_post, w_in, conv_w, conv_b, lru_w_a, lru_b_a, lru_w_x,
          lru_b_x, lru_lambda, rnn_out_norm, gla_w_gate, gla_b_gate, gla_out_norm, w_out,
          ffn_norm_pre, ffn_norm_post, w_ffn_gate, w_ffn_up, w_ffn_down, out):
    LAYERS, D, D_IN = w_in.shape
    SEQ = x.shape[1]
    D_FF = w_ffn_gate.shape[2]
    D_RNN = conv_w.shape[2]
    RANK, DK_ALL = gla_w_gate.shape[2:]
    DV = gla_out_norm.shape[1]
    HEADS = (D - D_RNN) // DV
    DK = DK_ALL // HEADS
    assert (x.shape[0], SEQ, D, D_RNN, DK, DV, RANK) == (1, 512, 1024, 512, 64, 128, 16)
    NC = D // P
    NS = SEQ // P
    NR = D_RNN // P
    NF = D_FF // P
    PAIRS = HEADS // 2
    NDP = 2 * PAIRS
    NCH = SEQ // CHUNK
    LAST = LAYERS - 1

    q0 = 2 * D_RNN
    v0 = q0 + 2 * DK_ALL
    g0 = v0 + HEADS * DV
    XR, LR, QK, V, G, GR = 0, NR, NR + 1, NR + 5, NR + 9, NR + 13
    IN_COLS = [c * P for c in range(NR)] + [D_IN - P] + [q0 + c * P for c in range(4)] \
        + [v0 + c * P for c in range(HEADS)] + [g0 + c * P for c in range(HEADS)] \
        + [D_RNN + c * P for c in range(NR)]
    B_OUT = len(IN_COLS)
    B_FF = B_OUT + NC
    B_DOWN = B_FF + 2 * NF
    DOWN_UNITS = [8, 8, NF - 16]
    NB = B_DOWN + 3 * NC
    RAW, SPL = 2, 4
    GAP = SPL - 1
    assert B_OUT % SPL == 1 and NC % SPL == 0 and (2 * NF) % SPL == 0 and (3 * NC) % SPL == 0

    def slot(b, ring):
        return (b if b < B_OUT else b + GAP) % ring

    def loads_before(b):
        return sum(slot(a, RAW) == slot(b, RAW) for a in range(b))

    LOADS = [sum(slot(a, RAW) == s for a in range(NB)) for s in range(RAW)]

    def free_after(b, ring):
        return b if b == B_OUT else b - ring + 1

    rows = {}
    n_rows = 0
    for name, n in (("mix_pre", NC), ("mix_post", NC), ("ffn_pre", NC), ("ffn_post", NC),
                    ("conv_w", 4 * NR), ("conv_b", NR), ("b_a", 2 * NR), ("b_x", 2 * NR),
                    ("lam", 2 * NR), ("rnn_norm", NR), ("gla_b", NDP), ("gla_norm", 1)):
        rows[name] = n_rows
        n_rows += n
    COL_TANH = n_rows
    COL_EXP = n_rows + 2 * NR
    n_cols = n_rows + 4 * NR

    ctx = ExitStack()
    with ctx:
        def sb(name, shape, dt=F32, stack=ctx):
            return stack.enter_context(nc.sbuf_tensor(name, shape, dt))

        def sem(name):
            return ctx.enter_context(nc.semaphore(name))

        def signal(name, per_layer, before=0):
            return Signal(sem(name), per_layer, before)

        xT = sb("xT", [P, NC, SEQ])
        h_hi = sb("h_hi", [P, NC, SEQ], F32R)
        h_lo = sb("h_lo", [P, NC, SEQ], F32R)
        raw = sb("raw", [P, RAW, 8 * P])
        w_hi = sb("w_hi", [P, SPL, 8 * P], F32R)
        w_lo = sb("w_lo", [P, SPL, 8 * P], F32R)
        sq = sb("sq", [P, 2, SEQ])
        y32 = sb("y32", [P, 2, SEQ])
        carrier = sb("carrier", [P, 2 * HEADS])
        started = sb("started", [P, 1])
        begun = sb("begun", [P, 4])
        rstd = sb("rstd", [P, SEQ])
        rstd_h = sb("rstd_h", [P, SEQ])
        reset = sb("reset", [P, SEQ], BF16)
        ident = sb("ident", [P, P])
        ones = sb("ones", [P, P])
        mask = sb("mask", [P, 2, P], U8)
        pcol = sb("pcol", [P, LAYERS, n_cols])
        par = sb("par", [P, n_cols])
        pre_gain = sb("pre_gain", [P, LAYERS + 1, NC])
        next_gain = sb("next_gain", [P, NC])
        decay = sb("decay", [P, NDP, NCH])

        with ExitStack() as region:
            mix = sb("mix", [P, 2 * NF + NC, SEQ], F32, region)
        g_hi = sb("g_hi", [P, NF, SEQ], F32R)
        g_lo = sb("g_lo", [P, NF, SEQ], F32R)
        m = sb("m", [P, NC, SEQ])

        def at(first, n):
            return mix[:, first:first + n, :]

        x_r = at(0, 4)
        rnn_r, rnn_i, rnn_t = at(0, 8), at(8, 8), at(16, 8)
        states = at(16, 7).rearrange("p t s -> p (t s)").rearrange(
            "p (k j v) -> p k j v", k=NDP, j=NCH - 1)
        scores = at(0, 4)
        xc = at(24, 4)
        y_rnn = xc
        qk = at(28, 4)
        gate_r = qk
        ke = at(32, 4)
        vT = ke
        lr, gla_w = mix[96:P, 32, :], mix[96:P, 33, :]
        qe = at(36, 4)
        kdec = at(40, 4)
        kdT = kdec.rearrange("p k (t d) -> p k t d", t=NS)
        v = at(44, 4)
        lru_w = at(44, 4).rearrange("p t s -> p (t s)").rearrange(
            "p (g r t j) -> p g r t j", g=2, r=2, t=NR)
        sg = at(48, 4)
        xs = at(0, 8).rearrange("p t s -> p (t s)").rearrange("p (t d) -> p t d", t=NS)
        mask32 = mix[:, 8, 0:2 * P].rearrange("p (d i) -> p d i", d=2)
        prow = mix[0:n_rows, 9, 0:LAYERS * P].rearrange("r (l p) -> r l p", l=LAYERS)
        sp = mix[:, 10, 0:8 * LAYERS * 2 * NR].rearrange("p (n l k) -> p n l k", n=8, l=LAYERS)

        bank = [ctx.enter_context(nc.psum_tensor(f"bank{i}", [P, SEQ], F32)) for i in range(8)]
        X_BANKS = [4, 5]
        FIRST = [0, 1, 2, 3]
        IN_BANKS = FIRST + [4, 5] + (B_OUT - 6) * [0, 1]
        LRU_BANKS = [2, 3, 4, 5]
        T_BANKS = [6, 2, 3, 4]
        U_BANKS = [[2, 3], [4, 5]]
        S_BANKS = [[0, 1], [2, 3]]
        O_BANKS = [6, 4, 5, 0]
        OUT_BANKS = [2, 3, 4, 5]
        DOWN_BANKS = [4, 5]

        def out_bank(c):
            return OUT_BANKS[c % len(OUT_BANKS)]

        STAT = 7

        loaded = [Signal(sem(f"loaded{s}"), 16 * LOADS[s]) for s in range(RAW)]
        hi_made = signal("hi_made", NB)
        lo_made = signal("lo_made", NB, RAW)
        block_used = signal("block_used", NB, SPL)
        s_gain, s_par, s_out = sem("s_gain"), sem("s_par"), sem("s_out")
        s_x = [sem(f"s_x{n}") for n in range(NC // 2)]
        lru_loaded, gla_loaded = signal("lru_loaded", 4 * 16), signal("gla_loaded", 2 * 16)
        const_made, masks_made = sem("const_made"), sem("masks_made")
        gain_turned, par_turned, pcol_made, gain_made, sp_step, sp_exp = (
            sem(n) for n in ("gain_turned", "par_turned", "pcol_made", "gain_made", "sp_step", "sp_exp"))
        x_turned, y_turned, x_odd, y_even, y_odd = (
            sem(n) for n in ("x_turned", "y_turned", "x_odd", "y_even", "y_odd"))
        par_made, lru_zeroed, scores_zeroed = signal("par_made", 2), signal("lru_zeroed", 2), signal("scores_zeroed", 1)
        x_made = signal("x_made", 2 * NC, NC)
        SQ_RNN, SQ_HEAD, SQ_POST, SQ_POST1, N_SQ = 0, 4, 8, 16, 24
        sq_made = signal("sq_made", N_SQ)
        xsq_made, xacc_made = signal("xsq_made", 2 * NC, NC), signal("xacc_made", 2 * (NC - 1), NC - 1)
        ST_HEAD, ST_POST, ST_PRE1, ST_POST1, N_ST = 2, 6, 8, 9, 11
        stat_mm = signal("stat_mm", N_ST)
        stat_read, rstd_made = signal("stat_read", 9, 1), signal("rstd_made", 9)
        H_Y, H_X1, H_X2 = 0, NC, 2 * NC
        y32_made, y_hi, y_lo = signal("y32_made", NC), signal("y_hi", 3 * NC, NC), signal("y_lo", 3 * NC, NC)
        head_scaled = signal("head_scaled", HEADS)
        m_made, m_scaled, acc_made = signal("m_made", 16, 2), signal("m_scaled", 16), signal("acc_made", 2 * (NC - 1))
        gate_scaled, silu_made, up_scaled, g32_made = (
            signal(n, NF) for n in ("gate_scaled", "silu_made", "up_scaled", "g32_made"))
        ghi_made, glo_made = signal("ghi_made", NF), signal("glo_made", NF)
        conv_step, in_made = signal("conv_step", 4 * NR), signal("in_made", B_OUT)
        lru_mm, lru_sig, tanh_made = signal("lru_mm", 16), signal("lru_sig", 16), signal("tanh_made", 8)
        z_mm, z_abs, z_min, z_exp, z_log = (
            signal(n, NDP, 1) for n in ("z_mm", "z_abs", "z_min", "z_exp", "z_log"))
        r_exp = signal("r_exp", 8)
        la_made, b_made = signal("la_made", NDP), signal("b_made", NDP)
        eb_made, enb_made = signal("eb_made", NDP), signal("enb_made", NDP)
        decay_made, qe_made, ke_made, kdec_made = (
            signal(n, NDP) for n in ("decay_made", "qe_made", "ke_made", "kdec_made"))
        v_turned, v_made, kd_turned, kd_made = (
            signal(n, 4) for n in ("v_turned", "v_made", "kd_turned", "kd_made"))
        rnn_q, rnn_xi, rnn_a, root_made, rnn_beta = (
            signal(n, 2) for n in ("rnn_q", "rnn_xi", "rnn_a", "root_made", "rnn_beta"))
        rnn_u = [signal(f"rnn_u{d}", 1) for d in range(2)]
        yacc_made = signal("yacc_made", NR - 1)
        scan_made = signal("scan_made", 8)
        hsum_made, yrnn_made, sgate_made, gelu_made = (
            signal(n, 1) for n in ("hsum_made", "yrnn_made", "sgate_made", "gelu_made"))
        u_mm, state_made = signal("u_mm", NDP), signal("state_made", NDP * (NCH - 1))
        score_mm, score_kept, o_mm = signal("score_mm", 8), signal("score_kept", 8), signal("o_mm", HEADS)

        def chunk_of(d, j):
            return j if d == 0 else NCH - 1 - j

        block = ctx.enter_context(nc.Block())

        @block.sync
        def _(sp_eng):

            def load_block(l, b, s, src, units=8):
                gap = free_after(b, RAW) if isinstance(b, int) else b + (1 - RAW)
                sp_eng.wait_ge(lo_made.sem, lo_made.after(l, gap))
                sp_eng.dma_start(raw[:, s, 0:units * P].rearrange("p (k c) -> p k c", k=units),
                                 src).then_inc(loaded[s].sem, 16)

            def cols(w, l, c):
                return w[l, :, bass.ds(c, P)].rearrange("(k p) c -> p k c", p=P)

            def first_block(l, layer, b):
                load_block(l, b, slot(b, RAW), cols(w_in, layer, IN_COLS[b]))

            def load_x(n):
                part = slice(n * 2 * P, (n + 1) * 2 * P)
                sp_eng.dma_start(xs[:, :, part], x[0, :, part].rearrange("(t p) d -> p t d", p=P)) \
                    .then_inc(s_x[n], 16)

            for b in range(RAW):
                first_block(0, 0, b)
            for n in range(NC // 2 - 1):
                load_x(n)
            first_block(0, 0, RAW)
            load_x(NC // 2 - 1)
            for b in range(RAW + 1, SPL):
                first_block(0, 0, b)
            for name, src in (("mix_post", mix_norm_post),
                              ("ffn_pre", ffn_norm_pre), ("ffn_post", ffn_norm_post),
                              ("conv_b", conv_b), ("rnn_norm", rnn_out_norm), ("gla_norm", gla_out_norm)):
                n = src.shape[1] // P
                sp_eng.dma_start(prow[rows[name]:rows[name] + n, :, :],
                                 src.rearrange("l (t p) -> t l p", p=P)).then_inc(s_par, 16)
            for name, src in (("conv_w", conv_w), ("b_a", lru_b_a), ("b_x", lru_b_x),
                              ("lam", lru_lambda), ("gla_b", gla_b_gate)):
                n = src.shape[1] * src.shape[2] // P
                sp_eng.dma_start(prow[rows[name]:rows[name] + n, :, :],
                                 src.rearrange("l w (t p) -> (w t) l p", p=P)).then_inc(s_par, 16)


            with sp_eng.Fori(0, LAYERS) as l:
                for b in range(SPL, QK + 2):
                    load_block(l, b, slot(b, RAW), cols(w_in, l, IN_COLS[b]))
                sp_eng.wait_ge(lru_zeroed.sem, lru_zeroed.after(l, 2))
                for g, w in enumerate((lru_w_a, lru_w_x)):
                    for odd in range(2):
                        src = w[l].rearrange("r (t q) i j -> q i (r t) j", q=2)[odd]
                        dst = lru_w.rearrange("p g r t j -> p g (r t) j")
                        sp_eng.dma_start(dst[64 * odd:64 * odd + 64, g, :, 64 * odd:64 * odd + 64],
                                         src).then_inc(lru_loaded.sem, 16)
                for d in range(2):
                    sp_eng.dma_start(mix[96 + RANK * d:96 + RANK * (d + 1), 33, d * DK_ALL:(d + 1) * DK_ALL],
                                     gla_w_gate[l, d]).then_inc(gla_loaded.sem, 16)
                for b in range(QK + 2, B_OUT):
                    load_block(l, b, slot(b, RAW), cols(w_in, l, IN_COLS[b]))
                for c in range(NC):
                    load_block(l, B_OUT + c, slot(B_OUT + c, RAW), cols(w_out, l, c * P))
                with sp_eng.Fori(0, NF // 2) as i:
                    for j in range(2):
                        load_block(l, i * 4 + (B_FF + 2 * j), 0, cols(w_ffn_gate, l, i * (2 * P) + j * P))
                        load_block(l, i * 4 + (B_FF + 2 * j + 1), 1, cols(w_ffn_up, l, i * (2 * P) + j * P))
                for c in range(NC):
                    k = 0
                    for j, units in enumerate(DOWN_UNITS):
                        b = B_DOWN + 3 * c + j
                        load_block(l, b, slot(b, RAW), w_ffn_down[l, k * P:(k + units) * P, bass.ds(c * P, P)]
                                   .rearrange("(k p) c -> p k c", p=P), units)
                        k += units
                with sp_eng.If(l < LAYERS - 1):
                    layer = nc.s_assert_within(
                        l + 1, 1, LAST, skip_runtime_bounds_check_because="the last layer is left out")
                    for b in range(SPL):
                        first_block(l + 1, layer, b)

            for half in range(2):
                for t in range(NS):
                    sp_eng.wait_ge(y_odd if t % 2 else y_even, half * NS // 2 + t // 2 + 1)
                    sp_eng.dma_start(out[0, t * P:(t + 1) * P, half * 512:(half + 1) * 512],
                                     xs[:, t, half * 512:(half + 1) * 512]).then_inc(s_out, 16)
            sp_eng.wait_ge(s_out, 16 * 2 * NS)

        @block.gpsimd
        def _(pool):
            pool.memset(started[:], 0.0).then_inc(lo_made.sem, RAW)
            pool.memset(ones[:], 1.0).then_inc(const_made, 1)
            pool.memset(ident[:], 0.0).then_inc(const_made, 1)
            pool.memset(pre_gain[:, LAYERS, :], 0.0).then_inc(const_made, 1)
            pool.memset(reset[:], 1.0).then_inc(const_made, 1)
            pool.memset(mask32, 1.0).then_inc(const_made, 1)
            pool.wait_ge(const_made, 5)
            pool.affine_select(out=ident[:], in_=ident[:], compare_op=ALU.not_equal, fill=1.0, base=0,
                               pattern=[[-1, P]], channel_multiplier=1).then_inc(const_made, 1)
            pool.memset(reset[:].rearrange("p (n t) -> p n t", t=CHUNK)[:, :, 0:1], 0.0).then_inc(const_made, 1)
            for d in range(2):
                pool.affine_select(out=mask32[:, d, :], in_=mask32[:, d, :], compare_op=ALU.is_ge, fill=0.0, base=0,
                                   pattern=[[1 - 2 * d, P]], channel_multiplier=2 * d - 1).then_inc(const_made, 1)
            pool.wait_ge(const_made, 9)
            for d in range(2):
                pool.memset(mask32[64 * d:64 * d + 64, d, 64 * (1 - d):64 * (1 - d) + 64], 0.0).then_inc(const_made, 1)

            pool.wait_ge(const_made, 11)

            def rest(l, b, b_slot, s, units=8):
                pool.wait_ge(hi_made.sem, hi_made.after(l, b + 1))
                pool.wait_ge(block_used.sem, block_used.after(l, b_slot))
                pool.tensor_tensor(w_lo[:, s, 0:units * P], raw[:, s % RAW, 0:units * P],
                                   w_hi[:, s, 0:units * P].bitcast(F32), ALU.subtract).then_inc(lo_made.sem, 1)

            def rest_of(l, b, units=8):
                rest(l, b, free_after(b, SPL), slot(b, SPL), units)

            def sum_squares(l, n_sq, n_acc):
                for c in range(1, NC):
                    pool.wait_ge(xsq_made.sem, xsq_made.after(l, n_sq + c + 1))
                    if c > 1:
                        pool.wait_ge(xacc_made.sem, xacc_made.after(l, n_acc + c - 1))
                    pool.tensor_tensor(y32[:, 0, :], sq[:, 0, :] if c == 1 else y32[:, 0, :], sq[:, c % 2, :],
                                       ALU.add).then_inc(xacc_made.sem, 1)

            def first_blocks(l):
                for b in range(SPL):
                    rest_of(l, b)

            first_blocks(0)
            sum_squares(0, -NC, 1 - NC)
            with pool.Fori(0, LAYERS) as l:
                for b in range(SPL, B_OUT + 2):
                    rest_of(l, b)
                    if b in (V + 3, V + 4):
                        d = b - (V + 3)
                        pool.wait_ge(lru_sig.sem, lru_sig.after(l, 16))
                        i = rnn_i[:, d * NR:(d + 1) * NR, :]
                        pool.tensor_tensor(i, i, xc, ALU.mult).then_inc(rnn_xi.sem, 1)
                    if b == B_OUT - 1:
                        i, beta = rnn_i[:, 0:NR, :], rnn_t[:, 0:NR, :]
                        pool.wait_ge(rnn_beta.sem, rnn_beta.after(l, 1))
                        pool.wait_ge(rnn_xi.sem, rnn_xi.after(l, 1))
                        pool.tensor_tensor(i, i, beta, ALU.mult).then_inc(rnn_u[0].sem, 1)
                for c in range(1, NR):
                    pool.wait_ge(sq_made.sem, sq_made.after(l, SQ_RNN + c + 1))
                    if c > 1:
                        pool.wait_ge(yacc_made.sem, yacc_made.after(l, c - 1))
                    pool.tensor_tensor(y32[:, 0, :], sq[:, 0, :] if c == 1 else y32[:, 0, :], sq[:, c % 2, :],
                                       ALU.add).then_inc(yacc_made.sem, 1)
                for b in range(B_OUT + 2, B_OUT + NC + SPL):
                    rest_of(l, b)
                sum_squares(l, 0, 0)
                with pool.Fori(1, NF // 2) as i:
                    for j in range(4):
                        b = i * 4 + (B_FF + j)
                        rest(l, b, b + (1 - SPL), j)
                for b in range(B_DOWN, NB):
                    rest_of(l, b, DOWN_UNITS[(b - B_DOWN) % 3])
                with pool.If(l < LAYERS - 1):
                    first_blocks(l + 1)
                    sum_squares(l, NC, NC - 1)

            for c in range(1, NC, 2):
                pool.wait_ge(m_scaled.sem, m_scaled.after(LAST, NC + c + 1))
                pool.tensor_tensor(xT[:, c, :], xT[:, c, :], m[:, c, :], ALU.add).then_inc(x_odd, 1)

        @block.scalar
        def _(act):
            def head(l, b, s, n_loads, gap, units=8):
                ring = loaded[s % RAW]
                act.wait_ge(ring.sem, ring.after(l, n_loads * 16 + 16))
                act.wait_ge(block_used.sem, block_used.after(l, gap))
                act.activation(w_hi[:, s, 0:units * P], raw[:, s % RAW, 0:units * P],
                               ACT.Copy).then_inc(hi_made.sem, 1)

            def head_of(l, b, units=8):
                head(l, b, slot(b, SPL), loads_before(b), free_after(b, SPL), units)

            def inverse_rms(l, n, mms, features, dst=rstd):
                act.wait_ge(stat_mm.sem, stat_mm.after(l, mms))
                act.activation(dst[:], bank[STAT][:], ACT.Ln, bias=EPS, scale=1.0 / features) \
                    .then_inc(stat_read.sem, 1)
                act.wait_ge(stat_read.sem, stat_read.after(l, n + 1))
                act.activation(dst[:], dst[:], ACT.Exp, scale=-0.5).then_inc(rstd_made.sem, 1)

            def split_x(l, c, n_x, gain):
                act.wait_ge(x_made.sem, x_made.after(l, n_x + c + 1))
                act.activation(h_hi[:, c, :], xT[:, c, :], ACT.Copy, scale=gain).then_inc(y_hi.sem, 1)

            def square_x(l, c, n_acc):
                if c >= 2:
                    act.wait_ge(xacc_made.sem, xacc_made.after(l, n_acc + max(1, c - 2)))
                act.activation(sq[:, c % 2, :], xT[:, c, :], ACT.Square).then_inc(xsq_made.sem, 1)

            def split_and_square_x(l, n_x, n_acc, gain):
                for c in range(NC):
                    split_x(l, c, n_x, gain(c))
                    square_x(l, c, n_acc)

            def split_hi(l, c, n):
                act.wait_ge(y32_made.sem, y32_made.after(l, n + 1))
                act.activation(h_hi[:, c, :], y32[:, c % 2, :], ACT.Copy).then_inc(y_hi.sem, 1)

            def square_of_output(l, c, n_m, n_acc):
                act.wait_ge(m_made.sem, m_made.after(l, n_m + c + 1))
                if c >= 2:
                    act.wait_ge(acc_made.sem, acc_made.after(l, n_acc + c - 1))
                act.activation(sq[:, c % 2, :], m[:, c, :], ACT.Square).then_inc(sq_made.sem, 1)

            def square_of_last(l, psum, n_acc):
                act.wait_ge(block_used.sem, block_used.after(l, NB if n_acc else B_FF))
                act.wait_ge(acc_made.sem, acc_made.after(l, n_acc + NC - 2))
                act.activation(sq[:, (NC - 1) % 2, :], bank[psum][:], ACT.Square) \
                    .then_inc(sq_made.sem, 1)

            act.dma_start(prow[0:NC, :, :], mix_norm_pre.rearrange("l (t p) -> t l p", p=P)).then_inc(s_gain, 16)
            act.preload_act_table_set(EXP_LN)
            act.wait_ge(const_made, 1)
            for n, signalled in enumerate((stat_read, z_abs, z_exp, z_log)):
                act.activation(begun[:, n:n + 1], ones[:, 0:1], ACT.Copy).then_inc(signalled.sem, 1)
            for b in range(RAW):
                head_of(0, b)
            act.wait_ge(gain_made, 1)
            for c in range(NC):
                split_x(0, c, -NC, pre_gain[:, 0, c:c + 1])
                if c in (3, 6):
                    head_of(0, 2 if c == 3 else 3)
            for c in range(NC):
                square_x(0, c, 1 - NC)

            act.wait_ge(pcol_made, LAYERS)
            act.activation(sp[:, 0], pcol[:, :, rows["lam"]:rows["lam"] + 2 * NR], ACT.Abs).then_inc(sp_exp, 1)
            act.wait_ge(sp_exp, 1)
            act.activation(sp[:, 1], sp[:, 0], ACT.Exp, scale=-1.0).then_inc(sp_exp, 1)

            with act.Fori(0, LAYERS) as l:
                inverse_rms(l, 0, 1, D, rstd_h)
                for b in range(SPL, QK + 4 + SPL - 1):
                    head_of(l, b)

                act.wait_ge(par_made.sem, par_made.after(l, 2))
                for c in range(NR):
                    for d in range(2):
                        for g, (dst, col) in enumerate(((rnn_r, "b_a"), (rnn_i, "b_x"))):
                            n = 4 * c + 2 * d + g
                            act.wait_ge(lru_mm.sem, lru_mm.after(l, n + 1))
                            k = rows[col] + d * NR + c
                            act.activation(dst[:, d * NR + c, :], bank[LRU_BANKS[2 * d + g]][:], ACT.Sigmoid,
                                           bias=par[:, k:k + 1]).then_inc(lru_sig.sem, 1)
                act.wait_ge(lru_sig.sem, lru_sig.after(l, 16))
                for n in range(2 * NR):
                    act.activation(rnn_t[:, n, :], rnn_r[:, n, :], ACT.Tanh,
                                   scale=par[:, COL_TANH + n:COL_TANH + n + 1]).then_inc(tanh_made.sem, 1)
                head_of(l, V + 3)

                for k in range(NDP):
                    act.wait_ge(z_min.sem, z_min.after(l, k + 1))
                    act.activation(qe[:, k, :], bank[T_BANKS[k]][:], ACT.Abs,
                                   bias=par[:, rows["gla_b"] + k:rows["gla_b"] + k + 1]).then_inc(z_abs.sem, 1)
                act.preload_act_table_set(EXP_LN)
                act.wait_ge(z_abs.sem, z_abs.after(l, NDP))
                act.activation(qe, qe, ACT.Exp, scale=-1.0).then_inc(z_exp.sem, NDP)
                head_of(l, V + 4)
                act.wait_ge(z_exp.sem, z_exp.after(l, NDP))
                act.activation(qe, qe, ACT.Ln, bias=1.0).then_inc(z_log.sem, NDP)
                act.wait_ge(tanh_made.sem, tanh_made.after(l, 8))
                for n in range(NR):
                    act.activation(rnn_r[:, n, :], rnn_r[:, n, :], ACT.Exp,
                                   scale=par[:, COL_EXP + n:COL_EXP + n + 1]).then_inc(r_exp.sem, 1)
                head_of(l, V + 5)
                for n in range(NR, 2 * NR):
                    act.activation(rnn_r[:, n, :], rnn_r[:, n, :], ACT.Exp,
                                   scale=par[:, COL_EXP + n:COL_EXP + n + 1]).then_inc(r_exp.sem, 1)
                head_of(l, V + 6)
                head_of(l, V + 7)

                for k in range(NDP):
                    act.wait_ge(b_made.sem, b_made.after(l, k + 1))
                    act.activation(qe[:, k, :], kdec[:, k, :], ACT.Exp, scale=1.0 / TAU).then_inc(eb_made.sem, 1)
                    if k == 0:
                        act.wait_ge(v_turned.sem, v_turned.after(l, 4))
                    act.activation(ke[:, k, :], kdec[:, k, :], ACT.Exp, scale=-1.0 / TAU).then_inc(enb_made.sem, 1)
                    if k == 1:
                        head_of(l, G + 4)
                head_of(l, G + 5)
                for d in range(2):
                    act.wait_ge(rnn_q.sem, rnn_q.after(l, d + 1))
                    act.activation(rnn_t[:, d * NR:(d + 1) * NR, :], rnn_t[:, d * NR:(d + 1) * NR, :],
                                   ACT.Sqrt).then_inc(root_made.sem, 1)
                    head_of(l, G + 6 + d)
                act.wait_ge(in_made.sem, in_made.after(l, GR))
                act.activation(sg, sg, ACT.Silu).then_inc(sgate_made.sem, 1)
                act.wait_ge(in_made.sem, in_made.after(l, B_OUT))
                act.activation(gate_r, gate_r, ACT.Gelu_apprx_tanh).then_inc(gelu_made.sem, 1)
                head_of(l, B_OUT)
                head_of(l, B_OUT + 1)

                act.preload_act_table_set(EXP_LN)

                act.wait_ge(yrnn_made.sem, yrnn_made.after(l, 1))
                for c in range(NR):
                    if c >= 2:
                        act.wait_ge(yacc_made.sem, yacc_made.after(l, max(1, c - 2)))
                    act.activation(sq[:, c % 2, :], y_rnn[:, c, :], ACT.Square).then_inc(sq_made.sem, 1)
                inverse_rms(l, 1, ST_HEAD, D_RNN)
                head_of(l, B_OUT + 2)
                head_of(l, B_OUT + 3)
                def square_of_head(h):
                    act.wait_ge(o_mm.sem, o_mm.after(l, h + 1))
                    act.activation(sq[:, h % 2, :], bank[O_BANKS[h]][:], ACT.Square).then_inc(sq_made.sem, 1)

                square_of_head(0)
                square_of_head(1)
                for c in range(NR):
                    split_hi(l, c, c)
                for h in range(HEADS):
                    if h:
                        act.wait_ge(head_scaled.sem, head_scaled.after(l, h))
                    else:
                        act.wait_ge(y32_made.sem, y32_made.after(l, NR))
                    inverse_rms(l, 2 + h, ST_HEAD + h + 1, DV)
                    if h:
                        split_hi(l, NR + h - 1, NR + h - 1)
                    if h + 2 < HEADS:
                        square_of_head(h + 2)
                split_hi(l, NC - 1, NC - 1)

                for c in range(NC):
                    head_of(l, B_OUT + c + SPL)
                    square_of_output(l, c, 0, 0) if c < NC - 1 else square_of_last(l, out_bank(c), 0)
                inverse_rms(l, 6, ST_POST + 2, D)

                split_and_square_x(l, 0, 0, lambda c: par[:, rows["ffn_pre"] + c:rows["ffn_pre"] + c + 1])
                inverse_rms(l, 7, ST_PRE1 + 1, D, rstd_h)

                act.preload_act_table_set(SILU)
                with act.Fori(0, NF // 2) as i:
                    for j in range(2):
                        f = i * 2 + j
                        b = i * 4 + (B_FF + SPL + 2 * j)
                        loads = [i * 2 + loads_before(B_FF + SPL + 2 * j + n) for n in range(2)]
                        head(l, b, 2 * j, loads[0], b + (1 - SPL))
                        act.wait_ge(gate_scaled.sem, gate_scaled.after(l, f + 1))
                        act.activation(sq[:, j, :], sq[:, j, :], ACT.Silu).then_inc(silu_made.sem, 1)
                        head(l, b + 1, 2 * j + 1, loads[1], b + (2 - SPL))
                        act.wait_ge(g32_made.sem, g32_made.after(l, f + 1))
                        act.activation(g_hi[:, bass.ds(f, 1), :], y32[:, j:j + 1, :], ACT.Copy) \
                            .then_inc(ghi_made.sem, 1)
                for b in range(B_DOWN + SPL, NB):
                    head_of(l, b, DOWN_UNITS[(b - B_DOWN) % 3])
                    c, n = divmod(b - SPL - B_DOWN, 3)
                    if n == 2:
                        square_of_output(l, c, NC, NC - 1)
                act.preload_act_table_set(EXP_LN)
                with act.If(l < LAYERS - 1):
                    head_of(l + 1, 0)
                square_of_output(l, NC - 2, NC, NC - 1)
                with act.If(l < LAYERS - 1):
                    head_of(l + 1, 1)
                    head_of(l + 1, 2)
                square_of_last(l, DOWN_BANKS[(NC - 1) % 2], NC - 1)
                with act.If(l < LAYERS - 1):
                    head_of(l + 1, 3)
                inverse_rms(l, 8, N_ST, D)
                with act.If(l < LAYERS - 1):
                    split_and_square_x(l, NC, NC - 1, lambda c: next_gain[:, c:c + 1])

            for half in range(2):
                act.wait_ge(y_turned, half + 1)
                for t in range(1, NS, 2):
                    act.activation(xs[:, t, half * 512:(half + 1) * 512], bank[NS * half + t][:], ACT.Copy) \
                        .then_inc(y_odd, 1)

        @block.tensor
        def _(pe):
            def keep_warm(n):
                for _ in range(n):
                    pe.matmul(bank[6][:, 0:P], ones[:], ones[:], start=True, stop=True)

            def passes(psum, s, unit, a_hi, a_lo, first, last):
                hi, lo = (w[:, s, unit * P:(unit + 1) * P] for w in (w_hi, w_lo))
                pe.matmul(psum, hi, a_hi, start=first, stop=False)
                pe.matmul(psum, hi, a_lo, start=False, stop=False)
                return pe.matmul(psum, lo, a_hi, start=False, stop=last)

            def project(l, b, s, psum, n_h=None):
                pe.wait_ge(lo_made.sem, lo_made.after(l, b + 1))
                if n_h is not None:
                    pe.wait_ge(y_lo.sem, y_lo.after(l, n_h))
                for k in range(NC):
                    last = passes(bank[psum][:], s, k, h_hi[:, k, :], h_lo[:, k, :], k == 0, k == NC - 1)
                last.then_inc(block_used.sem, 1)

            def project_first(l, b, n_h, n_acc, n_read):
                early = NC - 2
                for k in range(early):
                    pe.wait_ge(y_lo.sem, y_lo.after(l, n_h + k + 1))
                    for n in range(SPL):
                        if k == 0:
                            pe.wait_ge(lo_made.sem, lo_made.after(l, b + n + 1))
                        passes(bank[FIRST[n]][:], n, k, h_hi[:, k, :], h_lo[:, k, :], k == 0, False)
                stat(l, n_read, y32[:, 0, :], xacc_made.sem, xacc_made.after(l, n_acc), True, True)
                pe.wait_ge(y_lo.sem, y_lo.after(l, n_h + NC))
                for n in range(SPL):
                    for k in range(early, NC):
                        last = passes(bank[FIRST[n]][:], n, k, h_hi[:, k, :], h_lo[:, k, :], False, k == NC - 1)
                    last.then_inc(block_used.sem, 1)

            WARM = 22

            def stat(l, n_read, src, wait_sem, wait_value, first, last):
                if first:
                    pe.wait_ge(stat_read.sem, stat_read.after(l, n_read))
                pe.wait_ge(wait_sem, wait_value)
                pe.matmul(bank[STAT][:], ones[:], src, start=first, stop=last).then_inc(stat_mm.sem, 1)

            def turn4(dst, srcs, size=P):
                for i, src in enumerate(srcs):
                    last = pe.transpose(dst[:, i * P:(i + 1) * P], src, ident[:])
                return last

            pe.wait_ge(const_made, 1)
            pe.matmul(bank[6][:, 0:P], ones[:], ones[:], start=True, stop=True).then_inc(block_used.sem, SPL)
            pe.matmul(bank[6][:, 0:P], ones[:], ones[:], start=True, stop=True).then_inc(z_mm.sem, z_mm.before)
            pe.wait_ge(const_made, 6)
            pe.wait_ge(s_gain, 16)
            for l in range(LAYERS):
                last = pe.transpose(bank[STAT][:, l * NC:(l + 1) * NC], prow[0:NC, l, :], ident[0:NC, 0:NC])
            last.then_inc(gain_turned, 1)
            for c in range(NC):
                pe.wait_ge(s_x[c // 2], 16)
                if c >= 2:
                    pe.wait_ge(x_made.sem, c - 1)
                for t in range(NS):
                    last = pe.transpose(bank[X_BANKS[c % 2]][:, t * P:(t + 1) * P], xs[:, t, c * P:(c + 1) * P], ident[:])
                last.then_inc(x_turned, 1)
                keep_warm(1)
            pe.wait_ge(s_par, 16 * 11)
            for l in range(LAYERS):
                last = pe.transpose(bank[6][:, l * P:l * P + n_rows], prow[:, l, :], ident[0:n_rows, 0:n_rows])
            last.then_inc(par_turned, 1)

            with pe.Fori(0, LAYERS) as l:
                def project_in(b):
                    if b >= 6:
                        before = max(a for a in range(b) if IN_BANKS[a] == IN_BANKS[b])
                        pe.wait_ge(in_made.sem, in_made.after(l, before + 1))
                    project(l, b, slot(b, SPL), IN_BANKS[b])

                project_first(l, XR, -NC, 0, 0)
                for b in range(LR, V):
                    project_in(b)

                pe.wait_ge(lru_loaded.sem, lru_loaded.after(l, 64))
                for c in range(NR):
                    pe.wait_ge(conv_step.sem, conv_step.after(l, 4 * (c + 1)))
                    for d in range(2):
                        for g in range(2):
                            if c:
                                pe.wait_ge(lru_sig.sem, lru_sig.after(l, 4 * (c - 1) + 2 * d + g + 1))
                            pe.matmul(bank[LRU_BANKS[2 * d + g]][:], lru_w[:, g, d, c, :], xc[:, c, :],
                                      start=True, stop=True).then_inc(lru_mm.sem, 1)
                pe.wait_ge(gla_loaded.sem, gla_loaded.after(l, 32))
                for k in range(NDP):
                    d, pair = divmod(k, PAIRS)
                    if k:
                        pe.wait_ge(lru_sig.sem, lru_sig.after(l, 12 + k))
                    pe.matmul(bank[T_BANKS[k]][:], gla_w[:, d * DK_ALL + pair * P:d * DK_ALL + (pair + 1) * P], lr,
                              start=True, stop=True).then_inc(z_mm.sem, 1)

                for b in range(V, G):
                    project_in(b)
                pe.wait_ge(in_made.sem, in_made.after(l, G))
                pe.wait_ge(z_abs.sem, z_abs.after(l, NDP))
                for t in range(NS):
                    turn4(bank[T_BANKS[t]], [vT[:, c, t * P:(t + 1) * P] for c in range(HEADS)]) \
                        .then_inc(v_turned.sem, 1)
                for b in range(G, GR):
                    project_in(b)
                def turn_k_dec(k):
                    pe.wait_ge(kdec_made.sem, kdec_made.after(l, k + 1))
                    turn4(bank[T_BANKS[k]], [kdec[:, k, t * P:(t + 1) * P] for t in range(NS)]) \
                        .then_inc(kd_turned.sem, 1)

                def chunk_products(k):
                    d, pair = divmod(k, PAIRS)
                    if k == 0:
                        pe.wait_ge(kd_made.sem, kd_made.after(l, NDP))
                    if k >= 2:
                        pe.wait_ge(state_made.sem, state_made.after(l, (k - 1) * (NCH - 1)))
                    if k != 1:
                        pe.matmul(bank[6][:, 0:1], ones[:], ones[:, 0:1], start=True, stop=True)
                    for j in range(NCH - 1):
                        t, half = divmod(chunk_of(d, j), 2)
                        p0, c0 = CHUNK * half, j // 2 * DV
                        for odd in range(2):
                            last = pe.matmul(bank[U_BANKS[k % 2][j % 2]][DK * odd:DK * odd + DK, c0:c0 + DV],
                                             kdT[p0:p0 + CHUNK, k, t, DK * odd:DK * odd + DK],
                                             v[p0:p0 + CHUNK, t, (2 * pair + odd) * DV:(2 * pair + odd + 1) * DV],
                                             start=True, stop=True)
                    last.then_inc(u_mm.sem, 1)

                def score(h):
                    pair, odd = divmod(h, 2)
                    if h >= 2:
                        pe.wait_ge(score_kept.sem, score_kept.after(l, 2 * (h - 1)))
                    for d in range(2):
                        for t in range(NS):
                            a, b = (z[DK * odd:DK * odd + DK, d * PAIRS + pair, t * P:(t + 1) * P] for z in (ke, qe))
                            last = pe.matmul(bank[S_BANKS[odd][d]][:, t * P:(t + 1) * P], a, b, start=True, stop=True)
                        last.then_inc(score_mm.sem, 1)

                def output(h):
                    pair, odd = divmod(h, 2)
                    dst = bank[O_BANKS[h]]
                    pe.wait_ge(score_kept.sem, score_kept.after(l, 2 * h + 2))
                    for d in range(2):
                        for t in range(NS):
                            pe.matmul(dst[:, t * P:(t + 1) * P], v[:, t, h * DV:(h + 1) * DV],
                                      scores[:, 2 * d + h % 2, t * P:(t + 1) * P],
                                      start=(d == 0 and t == 0), stop=False, skip_group_check=True)
                    for d in range(2):
                        for j in range(NCH - 1):
                            i0 = chunk_of(d, j + 1) * CHUNK
                            last = pe.matmul(dst[:, i0:i0 + CHUNK],
                                             states[DK * odd:DK * odd + DK, d * PAIRS + pair, j, :],
                                             qe[DK * odd:DK * odd + DK, d * PAIRS + pair, i0:i0 + CHUNK],
                                             start=False, stop=(d == 1 and j == NCH - 2), skip_group_check=True)
                    last.then_inc(o_mm.sem, 1)

                def head_stat(h):
                    stat(l, 2 + h, sq[:, h % 2, :], sq_made.sem, sq_made.after(l, SQ_HEAD + h + 1), True, True)

                def project_out(b, ks):
                    for k in ks:
                        pe.wait_ge(y_lo.sem, y_lo.after(l, H_Y + k + 1))
                        last = passes(bank[out_bank(b - B_OUT)][:], slot(b, SPL), k, h_hi[:, k, :],
                                      h_lo[:, k, :], k == 0, k == NC - 1)
                    if k == NC - 1:
                        last.then_inc(block_used.sem, 1)

                pe.wait_ge(v_made.sem, v_made.after(l, NS))
                for k in range(NDP - 1):
                    turn_k_dec(k)
                project_in(GR)
                turn_k_dec(NDP - 1)
                project_in(GR + 1)
                chunk_products(0)
                project_in(GR + 2)
                chunk_products(1)
                project_in(GR + 3)
                chunk_products(2)
                pe.wait_ge(in_made.sem, in_made.after(l, B_OUT))
                score(0)
                chunk_products(3)
                pe.wait_ge(state_made.sem, state_made.after(l, 3 * (NCH - 1)))
                score(1)
                output(0)
                score(2)
                pe.wait_ge(state_made.sem, state_made.after(l, state_made.per_layer))
                output(1)
                stat(l, 1, y32[:, 0, :], yacc_made.sem, yacc_made.after(l, NR - 1), True, True)
                score(3)
                output(2)
                head_stat(0)
                head_stat(1)
                output(3)
                head_stat(2)
                for c in range(3):
                    pe.wait_ge(lo_made.sem, lo_made.after(l, B_OUT + c + 1))
                    if c == 2:
                        pe.wait_ge(head_scaled.sem, head_scaled.after(l, 2))
                    project_out(B_OUT + c, range(NR))
                    if c == 1:
                        head_stat(3)
                for c in range(3):
                    project_out(B_OUT + c, range(NR, NC))
                for b in range(B_OUT + 3, B_FF):
                    if b >= B_OUT + len(OUT_BANKS):
                        pe.wait_ge(m_made.sem, m_made.after(l, b - B_OUT - len(OUT_BANKS) + 1))
                    pe.wait_ge(lo_made.sem, lo_made.after(l, b + 1))
                    project_out(b, range(NC))
                stat(l, 6, y32[:, 0, :], acc_made.sem, acc_made.after(l, NC - 1), True, False)
                stat(l, 6, sq[:, (NC - 1) % 2, :], sq_made.sem, sq_made.after(l, SQ_POST + NC), False, True)
                keep_warm(WARM)

                project_first(l, B_FF, H_X1, NC - 1, 7)
                with pe.Fori(1, NF // 2) as i:
                    for j in range(2):
                        pe.wait_ge(gate_scaled.sem, gate_scaled.after(l, i * 2 + (j - 1)))
                        project(l, i * 4 + (B_FF + 2 * j), 2 * j, 2 * j)
                        pe.wait_ge(up_scaled.sem, up_scaled.after(l, i * 2 + (j - 1)))
                        project(l, i * 4 + (B_FF + 2 * j + 1), 2 * j + 1, 2 * j + 1)
                with pe.Fori(0, NC // 4) as i:
                    for j in range(4):
                        psum = DOWN_BANKS[j % 2]
                        pe.wait_ge(m_made.sem, m_made.after(l, i * 4 + (NC + j - 1)))
                        k = 0
                        for n, units in enumerate(DOWN_UNITS):
                            pe.wait_ge(lo_made.sem, lo_made.after(l, i * 12 + (B_DOWN + 3 * j + n + 1)))
                            pe.wait_ge(glo_made.sem, glo_made.after(l, k + units - (n == 2)))
                            for u in range(units):
                                if k == NF - 1:
                                    pe.wait_ge(glo_made.sem, glo_made.after(l, NF))
                                last = passes(bank[psum][:], (3 * j + n) % SPL, u, g_hi[:, k, :], g_lo[:, k, :],
                                              k == 0, k == NF - 1)
                                k += 1
                            last.then_inc(block_used.sem, 1)
                stat(l, 8, y32[:, 0, :], acc_made.sem, acc_made.after(l, 2 * (NC - 1)), True, False)
                stat(l, 8, sq[:, (NC - 1) % 2, :], sq_made.sem, sq_made.after(l, SQ_POST1 + NC), False, True)
                keep_warm(WARM)

            for c in range(NC):
                half, i = divmod(c, NC // 2)
                if c % 2:
                    pe.wait_ge(x_odd, c // 2 + 1)
                else:
                    pe.wait_ge(x_made.sem, x_made.after(LAST, NC + c // 2 + 1))
                for t in range(NS):
                    last = pe.transpose(bank[NS * half + t][:, i * P:(i + 1) * P], xT[:, c, t * P:(t + 1) * P], ident[:])
                if i == NC // 2 - 1:
                    last.then_inc(y_turned, 1)

        @block.vector
        def _(dve):
            def rest_of_x(l, c, n, gain):
                dve.wait_ge(y_hi.sem, y_hi.after(l, n + c + 1))
                dve.scalar_tensor_tensor(h_lo[:, c, :], xT[:, c, :], gain, h_hi[:, c, :].bitcast(F32),
                                         ALU.mult, ALU.subtract).then_inc(y_lo.sem, 1)

            dve.memset(carrier[:, 0:1], 0.0).then_inc(m_made.sem, 2)
            dve.memset(carrier[:, 2:3], 0.0).then_inc(z_min.sem, 1)
            dve.wait_ge(const_made, 11)
            dve.tensor_copy(mask[:], mask32).then_inc(masks_made, 1)
            dve.wait_ge(gain_turned, 1)
            dve.tensor_copy(pre_gain[:, 0:LAYERS, :],
                            bank[STAT][:, 0:LAYERS * NC].rearrange("p (l c) -> p l c", l=LAYERS)).then_inc(gain_made, 1)
            dve.wait_ge(gain_made, 1)
            for c in range(NC + 1):
                if c < NC:
                    dve.wait_ge(x_turned, c + 1)
                    dve.tensor_copy(xT[:, c, :], bank[X_BANKS[c % 2]][:]).then_inc(x_made.sem, 1)
                if c:
                    rest_of_x(0, c - 1, -NC, pre_gain[:, 0, c - 1:c])

            dve.wait_ge(par_turned, 1)
            for l in range(LAYERS):
                dve.tensor_copy(pcol[:, l, 0:n_rows], bank[6][:, l * P:l * P + n_rows]).then_inc(pcol_made, 1)

            done = [0]

            def step(ins):
                done[0] += 1
                ins.then_inc(sp_step, 1)
                dve.wait_ge(sp_step, done[0])

            lam = pcol[:, :, rows["lam"]:rows["lam"] + 2 * NR]
            dve.wait_ge(sp_exp, 2)
            step(dve.tensor_scalar(sp[:, 2], sp[:, 1], 2.0, None, ALU.add))
            step(dve.reciprocal(sp[:, 3], sp[:, 2]))
            step(dve.tensor_tensor(sp[:, 4], sp[:, 1], sp[:, 3], ALU.mult))
            step(dve.tensor_tensor(sp[:, 5], sp[:, 4], sp[:, 4], ALU.mult))
            step(dve.tensor_scalar(sp[:, 6], sp[:, 5], 1.0 / 19, None, ALU.mult))
            for odd in range(17, 1, -2):
                step(dve.scalar_tensor_tensor(sp[:, 6], sp[:, 6], 1.0 / odd, sp[:, 5], ALU.add, ALU.mult))
            step(dve.scalar_tensor_tensor(sp[:, 6], sp[:, 6], 1.0, sp[:, 4], ALU.add, ALU.mult))
            step(dve.tensor_scalar(sp[:, 7], lam, -1.0, 0.0, ALU.mult, ALU.max))
            step(dve.scalar_tensor_tensor(sp[:, 7], sp[:, 6], 2.0, sp[:, 7], ALU.mult, ALU.add))
            dve.tensor_scalar(pcol[:, :, COL_TANH:COL_TANH + 2 * NR], sp[:, 7], LRU_C / 2, None,
                              ALU.mult).then_inc(pcol_made, 1)
            dve.tensor_scalar(pcol[:, :, COL_EXP:COL_EXP + 2 * NR], sp[:, 7], -LRU_C, None,
                              ALU.mult).then_inc(pcol_made, 1)
            dve.wait_ge(pcol_made, LAYERS + 2)
            dve.wait_ge(masks_made, 1)

            def col(name, k=0):
                k += rows[name]
                return par[:, k:k + 1]

            def split_lo(l, c, n):
                dve.wait_ge(y_hi.sem, y_hi.after(l, n + 1))
                dve.tensor_tensor(h_lo[:, c, :], y32[:, c % 2, :], h_hi[:, c, :].bitcast(F32),
                                  ALU.subtract).then_inc(y_lo.sem, 1)

            def normalise(l, n, chunks, src, gain, n_rstd):
                dve.wait_ge(rstd_made.sem, rstd_made.after(l, n_rstd + 1))
                for c in range(chunks):
                    if c >= 2:
                        dve.wait_ge(y_lo.sem, y_lo.after(l, n + c - 1))
                    dve.scalar_tensor_tensor(y32[:, c % 2, :], src[:, c, :], col(gain, c), rstd[:],
                                             ALU.mult, ALU.mult).then_inc(y32_made.sem, 1)
                    if c:
                        split_lo(l, c - 1, n + c - 1)
                split_lo(l, chunks - 1, n + chunks - 1)

            def take_output(l, c, b, psum, n, n_sq):
                dve.wait_ge(block_used.sem, block_used.after(l, b + 1))
                if c == NC - 1:
                    dve.wait_ge(sq_made.sem, sq_made.after(l, n_sq + NC))
                dve.tensor_copy(m[:, c, :], bank[psum][:]).then_inc(m_made.sem, 1)
                if c == NC - 1:
                    return
                dve.wait_ge(sq_made.sem, sq_made.after(l, n_sq + c + 1))
                if c == 0:
                    dve.tensor_copy(y32[:, 0, :], sq[:, 0, :]).then_inc(acc_made.sem, 1)
                else:
                    dve.wait_ge(acc_made.sem, acc_made.after(l, n + c))
                    dve.tensor_tensor(y32[:, 0, :], y32[:, 0, :], sq[:, c % 2, :], ALU.add).then_inc(acc_made.sem, 1)

            def scale_branch(c, gain):
                dve.scalar_tensor_tensor(m[:, c, :], m[:, c, :], col(gain, c), rstd[:], ALU.mult, ALU.mult) \
                    .then_inc(m_scaled.sem, 1)

            def add_to_x(l, c, n):
                dve.wait_ge(m_scaled.sem, m_scaled.after(l, n + c + 1))
                dve.tensor_tensor(xT[:, c, :], xT[:, c, :], m[:, c, :], ALU.add).then_inc(x_made.sem, 1)

            def add_branch(l, n, gain, n_rstd, n_h, h_gain):
                dve.wait_ge(rstd_made.sem, rstd_made.after(l, n_rstd + 1))
                dve.wait_ge(m_made.sem, m_made.after(l, n + NC))
                for c in range(NC + 1):
                    if c < NC:
                        scale_branch(c, gain)
                        add_to_x(l, c, n)
                    if c:
                        rest_of_x(l, c - 1, n_h, h_gain(c - 1))

            with dve.Fori(0, LAYERS) as l:
                dve.wait_ge(y_lo.sem, y_lo.after(l, 0))
                dve.tensor_copy(par[:].rearrange("p (o n) -> p o n", o=1), pcol[:, bass.ds(l, 1), :]) \
                    .then_inc(par_made.sem, 1)
                dve.tensor_copy(next_gain[:].rearrange("p (o n) -> p o n", o=1), pre_gain[:, bass.ds(l + 1, 1), :]) \
                    .then_inc(par_made.sem, 1)
                dve.memset(mix[96:P, 33, :], 0.0).then_inc(lru_zeroed.sem, 1)
                dve.memset(at(44, 4), 0.0).then_inc(lru_zeroed.sem, 1)

                def take_in(b, dst):
                    rows_ = slice(96, P) if b == LR else slice(0, P)
                    dve.wait_ge(block_used.sem, block_used.after(l, b + 1))
                    dve.tensor_tensor(dst, bank[IN_BANKS[b]][rows_, :], rstd_h[rows_, :],
                                      ALU.mult).then_inc(in_made.sem, 1)

                dve.wait_ge(rstd_made.sem, rstd_made.after(l, 1))
                for c in range(NR):
                    take_in(XR + c, x_r[:, c, :])
                take_in(LR, lr)

                dve.wait_ge(par_made.sem, par_made.after(l, 2))
                for c in range(NR):
                    dve.wait_ge(in_made.sem, in_made.after(l, XR + c + 1))
                    dve.tensor_scalar(xc[:, c, :], x_r[:, c, :], col("conv_w", 2 * NR + c), col("conv_b", c),
                                      ALU.mult, ALU.add).then_inc(conv_step.sem, 1)
                    for n, (tap, shift) in enumerate(((0, -2), (1, -1), (3, 1))):
                        lo, hi = max(0, -shift), SEQ - max(0, shift)
                        dve.wait_ge(conv_step.sem, conv_step.after(l, 4 * c + n + 1))
                        dve.scalar_tensor_tensor(xc[:, c, lo:hi], x_r[:, c, lo + shift:hi + shift],
                                                 col("conv_w", tap * NR + c), xc[:, c, lo:hi],
                                                 ALU.mult, ALU.add).then_inc(conv_step.sem, 1)
                    take_in(QK + c, qk[:, c, :])

                for k in range(NDP):
                    dve.wait_ge(z_mm.sem, z_mm.after(l, k + 1))
                    dve.tensor_scalar(kdec[:, k, :], bank[T_BANKS[k]][:], col("gla_b", k), 0.0,
                                      ALU.add, ALU.min).then_inc(z_min.sem, 1)
                take_in(V, vT[:, 0, :])
                dve.wait_ge(z_log.sem, z_log.after(l, NDP))
                dve.wait_ge(z_min.sem, z_min.after(l, NDP))
                for k in range(NDP):
                    dve.tensor_tensor(kdec[:, k, :], kdec[:, k, :], qe[:, k, :], ALU.subtract) \
                        .then_inc(la_made.sem, 1)
                for k in range(NDP):
                    dve.wait_ge(la_made.sem, la_made.after(l, k + 1))
                    seq = kdec[:, k, :] if k < PAIRS else kdec[:, k, ::-1]
                    dve.tensor_tensor_scan(seq, reset[:], seq, 0.0, ALU.mult, ALU.add).then_inc(b_made.sem, 1)
                    if k == 0:
                        take_in(V + 1, vT[:, 1, :])
                take_in(V + 2, vT[:, 2, :])

                def group(z, d):
                    return z[:, d * NR:(d + 1) * NR, :]

                for d in range(2):
                    dve.wait_ge(r_exp.sem, r_exp.after(l, NR * (d + 1)))
                    r, t = group(rnn_r, d), group(rnn_t, d)
                    dve.scalar_tensor_tensor(r, r, 1.0, t, ALU.add, ALU.mult).then_inc(rnn_q.sem, 1)
                    dve.wait_ge(rnn_q.sem, rnn_q.after(l, d + 1))
                    dve.tensor_scalar(r, r, -1.0, 1.0, ALU.mult, ALU.add).then_inc(rnn_a.sem, 1)
                    take_in(V + 3, vT[:, 3, :]) if d == 0 else take_in(G, sg[:, 0, :])

                for t in range(NS):
                    dve.wait_ge(v_turned.sem, v_turned.after(l, t + 1))
                    dve.tensor_copy(v[:, t, :], bank[T_BANKS[t]][:]).then_inc(v_made.sem, 1)

                def beta(d):
                    r, t = group(rnn_r, d), group(rnn_t, d)
                    dve.wait_ge(root_made.sem, root_made.after(l, d + 1))
                    dve.wait_ge(rnn_a.sem, rnn_a.after(l, d + 1))
                    dve.scalar_tensor_tensor(t, r, 1.0, t, ALU.add, ALU.mult).then_inc(rnn_beta.sem, 1)

                for k in range(NDP):
                    d, pair = divmod(k, PAIRS)
                    dve.wait_ge(eb_made.sem, eb_made.after(l, k + 1))
                    dve.wait_ge(enb_made.sem, enb_made.after(l, k + 1))
                    last = 0 if d else CHUNK - 1
                    dve.tensor_copy(decay[:, k, :], qe[:, k, :].rearrange("p (n t) -> p n t", t=CHUNK)[:, :, last]) \
                        .then_inc(decay_made.sem, 1)
                    dve.tensor_tensor(ke[:, k, :], qk[:, PAIRS + pair, :], ke[:, k, :], ALU.mult).then_inc(ke_made.sem, 1)
                    dve.wait_ge(decay_made.sem, decay_made.after(l, k + 1))
                    dve.scalar_tensor_tensor(qe[:, k, :], qk[:, pair, :], DK ** -0.5, qe[:, k, :],
                                             ALU.mult, ALU.mult).then_inc(qe_made.sem, 1)
                    dve.wait_ge(ke_made.sem, ke_made.after(l, k + 1))
                    chunks = [z[:, k, :].rearrange("p (n t) -> p n t", t=CHUNK) for z in (kdec, ke)]
                    dve.tensor_tensor(chunks[0], chunks[1],
                                      decay[:, k, :].rearrange("p (n o) -> p n o", o=1).to_broadcast([P, NCH, CHUNK]),
                                      ALU.mult).then_inc(kdec_made.sem, 1)
                    if k < 3:
                        take_in(G + 1 + k, sg[:, 1 + k, :])
                    if k == 2:
                        beta(0)

                def make_states(k):
                    dve.wait_ge(u_mm.sem, u_mm.after(l, k + 1))
                    for j in range(NCH - 1):
                        u = bank[U_BANKS[k % 2][j % 2]][:, j // 2 * DV:(j // 2 + 1) * DV]
                        c = chunk_of(k // PAIRS, j)
                        if j == 0:
                            last = dve.tensor_copy(states[:, k, j, :], u)
                        else:
                            dve.wait_ge(state_made.sem, state_made.after(l, k * (NCH - 1) + j))
                            last = dve.scalar_tensor_tensor(states[:, k, j, :], states[:, k, j - 1, :],
                                                            decay[:, k, c:c + 1], u, ALU.mult, ALU.add)
                        last.then_inc(state_made.sem, 1)

                def keep(h):
                    if h >= 2:
                        dve.wait_ge(o_mm.sem, o_mm.after(l, h - 1))
                    for d in range(2):
                        dve.wait_ge(score_mm.sem, score_mm.after(l, 2 * h + d + 1))
                        dve.tensor_copy(carrier[:, 2 * h + d:2 * h + d + 1], ones[:, 0:1])
                        dve.copy_predicated(scores[:, 2 * d + h % 2, :].rearrange("p (t i) -> p t i", t=NS),
                                            mask[:, d:d + 1, :].to_broadcast([P, NS, P]),
                                            bank[S_BANKS[h % 2][d]][:].rearrange("p (t i) -> p t i", t=NS)) \
                            .then_inc(score_kept.sem, 1)

                def scans(d):
                    dve.wait_ge(rnn_u[d].sem, rnn_u[d].after(l, 1))
                    for c in range(NR):
                        a, u = (z[:, d * NR + c, :] if d == 0 else z[:, d * NR + c, ::-1] for z in (rnn_r, rnn_i))
                        dve.tensor_tensor_scan(u, a, u, 0.0, ALU.mult, ALU.add).then_inc(scan_made.sem, 1)

                def take_k_dec(k):
                    dve.wait_ge(kd_turned.sem, kd_turned.after(l, k + 1))
                    dve.tensor_copy(kdT[:, k], bank[T_BANKS[k]][:].rearrange("p (t d) -> p t d", t=NS)) \
                        .then_inc(kd_made.sem, 1)

                for k in range(NDP - 1):
                    take_k_dec(k)
                beta(1)
                take_in(GR, gate_r[:, 0, :])
                take_k_dec(NDP - 1)
                dve.wait_ge(rnn_beta.sem, rnn_beta.after(l, 2))
                dve.wait_ge(rnn_xi.sem, rnn_xi.after(l, 2))
                dve.tensor_tensor(group(rnn_i, 1), group(rnn_i, 1), group(rnn_t, 1), ALU.mult) \
                    .then_inc(rnn_u[1].sem, 1)
                scans(0)
                take_in(GR + 1, gate_r[:, 1, :])
                make_states(0)
                scans(1)
                take_in(GR + 2, gate_r[:, 2, :])
                dve.memset(scores, 0.0).then_inc(scores_zeroed.sem, 1)
                make_states(1)
                dve.wait_ge(scan_made.sem, scan_made.after(l, 8))
                dve.tensor_tensor(group(rnn_i, 0), group(rnn_i, 0), group(rnn_i, 1), ALU.add).then_inc(hsum_made.sem, 1)
                take_in(GR + 3, gate_r[:, 3, :])
                make_states(2)
                dve.wait_ge(scores_zeroed.sem, scores_zeroed.after(l, 1))
                keep(0)
                make_states(3)
                keep(1)
                dve.wait_ge(hsum_made.sem, hsum_made.after(l, 1))
                dve.wait_ge(gelu_made.sem, gelu_made.after(l, 1))
                dve.tensor_tensor(y_rnn, group(rnn_i, 0), gate_r, ALU.mult).then_inc(yrnn_made.sem, 1)
                dve.wait_ge(block_used.sem, block_used.after(l, B_OUT))
                keep(2)
                keep(3)
                normalise(l, H_Y, NR, y_rnn, "rnn_norm", 1)
                dve.wait_ge(sgate_made.sem, sgate_made.after(l, 1))
                for h in range(HEADS):
                    n = H_Y + NR + h
                    dve.wait_ge(rstd_made.sem, rstd_made.after(l, 3 + h))
                    dve.wait_ge(y_lo.sem, y_lo.after(l, n - 1))
                    dve.scalar_tensor_tensor(y32[:, h % 2, :], bank[O_BANKS[h]][:], col("gla_norm"), rstd[:],
                                             ALU.mult, ALU.mult).then_inc(head_scaled.sem, 1)
                    dve.wait_ge(head_scaled.sem, head_scaled.after(l, h + 1))
                    dve.tensor_tensor(y32[:, h % 2, :], y32[:, h % 2, :], sg[:, h, :], ALU.mult) \
                        .then_inc(y32_made.sem, 1)
                    split_lo(l, NR + h, n)

                for c in range(NC):
                    take_output(l, c, B_OUT + c, out_bank(c), 0, SQ_POST)
                add_branch(l, 0, "mix_post", 6, H_X1, lambda c: col("ffn_pre", c))

                with dve.Fori(0, NF // 2) as i:
                    dve.wait_ge(rstd_made.sem, rstd_made.after(l, 8))
                    for j in range(2):
                        f = i * 2 + j
                        b = i * 4 + (B_FF + 2 * j)
                        dve.wait_ge(block_used.sem, block_used.after(l, b + 1))
                        dve.tensor_tensor(sq[:, j, :], bank[2 * j][:], rstd_h[:], ALU.mult) \
                            .then_inc(gate_scaled.sem, 1)
                        dve.wait_ge(block_used.sem, block_used.after(l, b + 2))
                        dve.tensor_tensor(y32[:, j, :], bank[2 * j + 1][:], rstd_h[:], ALU.mult) \
                            .then_inc(up_scaled.sem, 1)
                        dve.wait_ge(silu_made.sem, silu_made.after(l, f + 1))
                        dve.wait_ge(up_scaled.sem, up_scaled.after(l, f + 1))
                        dve.tensor_tensor(y32[:, j, :], sq[:, j, :], y32[:, j, :], ALU.mult) \
                            .then_inc(g32_made.sem, 1)
                        dve.wait_ge(ghi_made.sem, ghi_made.after(l, f + 1))
                        dve.tensor_tensor(g_lo[:, bass.ds(f, 1), :], y32[:, j:j + 1, :],
                                          g_hi[:, bass.ds(f, 1), :].bitcast(F32), ALU.subtract) \
                            .then_inc(glo_made.sem, 1)
                dve.wait_ge(glo_made.sem, glo_made.after(l, NF))
                for c in range(NC):
                    take_output(l, c, B_DOWN + 3 * c + 2, DOWN_BANKS[c % 2], NC - 1, SQ_POST1)
                with dve.If(l < LAYERS - 1):
                    add_branch(l, NC, "ffn_post", 8, H_X2, lambda c: next_gain[:, c:c + 1])

            dve.wait_ge(rstd_made.sem, rstd_made.after(LAST, 9))
            dve.wait_ge(m_made.sem, m_made.after(LAST, 2 * NC))
            for c in range(0, NC, 2):
                scale_branch(c, "ffn_post")
                scale_branch(c + 1, "ffn_post")
                add_to_x(LAST, c, NC)
            for half in range(2):
                dve.wait_ge(y_turned, half + 1)
                for t in range(0, NS, 2):
                    dve.tensor_copy(xs[:, t, half * 512:(half + 1) * 512], bank[NS * half + t][:]).then_inc(y_even, 1)


_INS = ['x', 'mix_norm_pre', 'mix_norm_post', 'w_in', 'conv_w', 'conv_b', 'lru_w_a', 'lru_b_a', 'lru_w_x',
        'lru_b_x', 'lru_lambda', 'rnn_out_norm', 'gla_w_gate', 'gla_b_gate', 'gla_out_norm', 'w_out',
        'ffn_norm_pre', 'ffn_norm_post', 'w_ffn_gate', 'w_ffn_up', 'w_ffn_down']


def kernel(**inputs):
    import numpy as np
    import concourse.bacc as bacc
    from concourse.bass_utils import run_bass_kernel_spmd

    nc = bacc.Bacc("TRN2", target_bir_lowering=False, num_devices=1)
    arrays, args = {}, []
    for name in _INS:
        a = np.ascontiguousarray(inputs[name])
        arrays[f"in_{name}"] = a
        args.append(nc.dram_tensor(f"in_{name}", a.shape, mybir.dt.from_np(a.dtype), kind="ExternalInput").ap())
    shape = arrays["in_x"].shape
    args.append(nc.dram_tensor("out_x", shape, F32, kind="ExternalOutput").ap())
    trunk(nc, *args)
    r = run_bass_kernel_spmd(nc, [arrays], core_ids=[0])
    return r.results[0]["out_x"]
```
